# Optimizing a Trainium2 kernel written in Bass

```python
import jax, jax.numpy as jnp
from jax import lax
import numpy as np

D_MODEL = 1024
BATCH = 1
SEQ = 512
DEPTH = 1

CHUNK = 64
Q_BLOCK = 128
EPS = 1e-6

POOL_WIDTH = D_MODEL // 4
POOL_WINDOWS = (2, 4, 8, 16)
POOL_GROUPS = len(POOL_WINDOWS)
POOL_GROUP = POOL_WIDTH // POOL_GROUPS
GLA_WIDTH = D_MODEL // 4
GLA_HEADS = 4
GLA_HEAD_DIM = GLA_WIDTH // GLA_HEADS
GLA_GATE_RANK = 16
GLA_TAU = 16.0
FOX_WIDTH = D_MODEL - POOL_WIDTH - GLA_WIDTH
FOX_HEAD_DIM = 64
FOX_HEADS = FOX_WIDTH // FOX_HEAD_DIM
D_FF = ((-(-8 * D_MODEL // 3)) + 255) // 256 * 256

IN_SIZES = (POOL_WIDTH,
            GLA_WIDTH, GLA_WIDTH, GLA_WIDTH, GLA_WIDTH,
            GLA_GATE_RANK,
            FOX_WIDTH, FOX_WIDTH, FOX_WIDTH,
            FOX_HEADS)
IN_WIDTH = sum(IN_SIZES)


def _split_points():
    pts, acc = [], 0
    for s in IN_SIZES[:-1]:
        acc += s
        pts.append(acc)
    return pts

def rmsnorm(x, g):
    x32 = x.astype(jnp.float32)
    y = x32 * lax.rsqrt(jnp.mean(x32 * x32, axis=-1, keepdims=True) + EPS) * g.astype(jnp.float32)
    return y.astype(x.dtype)

def pool_mixer(u, w_pool, pool_scale):
    B, T, _ = u.shape
    u32 = u.astype(jnp.float32)
    cs = jnp.cumsum(u32, axis=1)
    cs_pad = jnp.concatenate([jnp.zeros((B, 1, POOL_WIDTH), jnp.float32), cs], axis=1)
    t1 = jnp.arange(1, T + 1)
    means = []
    for gi, w in enumerate(POOL_WINDOWS):
        lo, hi = gi * POOL_GROUP, (gi + 1) * POOL_GROUP
        lagged = jnp.concatenate([jnp.zeros((B, w - 1, POOL_GROUP), jnp.float32),
                                  cs_pad[:, :T - w + 1, lo:hi]], axis=1)
        cnt = jnp.minimum(t1, w).astype(jnp.float32)
        means.append((cs[:, :, lo:hi] - lagged) / cnt[None, :, None])
    d = (jnp.concatenate(means, axis=-1) - u32).astype(u.dtype)
    d = d.reshape(B, T, POOL_GROUPS, POOL_GROUP)
    y = jnp.einsum('btgc,gcd->btgd', d, w_pool).reshape(B, T, POOL_WIDTH)
    return y * pool_scale

def gla_mixer(q, k, v, g, a_low, w_a_up, b_a, gla_gn):
    B, T, _ = q.shape
    H, Dh, C = GLA_HEADS, GLA_HEAD_DIM, CHUNK
    NC = T // C

    def heads(z):
        return z.astype(jnp.float32).reshape(B, NC, C, H, Dh).transpose(0, 3, 1, 2, 4)

    log_a = jax.nn.log_sigmoid(jnp.einsum('btr,rd->btd', a_low.astype(jnp.float32),
                                          w_a_up.astype(jnp.float32)) + b_a.astype(jnp.float32)) / GLA_TAU
    qh = heads(q) * (Dh ** -0.5)
    kh, vh, la = heads(k), heads(v), heads(log_a)
    bcum = jnp.cumsum(la, axis=3)
    b_last = bcum[:, :, :, -1:, :]
    ref = bcum[:, :, :, C // 2 - 1:C // 2, :]

    q_in = qh * jnp.exp(bcum - ref)
    k_in = kh * jnp.exp(ref - bcum)
    causal = jnp.tril(jnp.ones((C, C), dtype=bool))
    att = jnp.where(causal, jnp.einsum('bhncd,bhnsd->bhncs', q_in, k_in), 0.0)
    o_intra = jnp.einsum('bhncs,bhnse->bhnce', att, vh)

    kv = jnp.einsum('bhncd,bhnce->bhnde', kh * jnp.exp(b_last - bcum), vh)
    dec = jnp.exp(b_last[:, :, :, 0, :])

    def step(S, inp):
        kv_n, dec_n = inp
        return dec_n[..., None] * S + kv_n, S

    S0 = jnp.zeros((B, H, Dh, Dh), jnp.float32)
    _, S_prev = lax.scan(step, S0, (kv.transpose(2, 0, 1, 3, 4), dec.transpose(2, 0, 1, 3)))
    S_prev = S_prev.transpose(1, 2, 0, 3, 4)
    o_inter = jnp.einsum('bhncd,bhnde->bhnce', qh * jnp.exp(bcum), S_prev)

    o = o_intra + o_inter
    o = o * lax.rsqrt(jnp.mean(o * o, axis=-1, keepdims=True) + EPS)
    o = o.transpose(0, 2, 3, 1, 4).reshape(B, T, GLA_WIDTH) * gla_gn.astype(jnp.float32)
    return (o * jax.nn.silu(g.astype(jnp.float32))).astype(q.dtype)

def fox_mixer(q, k, v, f_logit, b_f):
    B, T, _ = q.shape
    H, Dh = FOX_HEADS, FOX_HEAD_DIM
    nb = T // Q_BLOCK

    def heads(z):
        return z.astype(jnp.float32).reshape(B, T, H, Dh).transpose(0, 2, 1, 3)

    qh = heads(q) * (Dh ** -0.5)
    kh, vh = heads(k), heads(v)
    logf = jax.nn.log_sigmoid(f_logit.astype(jnp.float32) + b_f.astype(jnp.float32))
    F = jnp.cumsum(logf, axis=1).transpose(0, 2, 1)
    q_blocks = qh.reshape(B, H, nb, Q_BLOCK, Dh).transpose(2, 0, 1, 3, 4)
    F_blocks = F.reshape(B, H, nb, Q_BLOCK).transpose(2, 0, 1, 3)
    kpos = jnp.arange(T)

    def block(args):
        qb, Fb, i = args
        s = jnp.einsum('bhqd,bhkd->bhqk', qb, kh) + Fb[..., None] - F[:, :, None, :]
        qpos = i * Q_BLOCK + jnp.arange(Q_BLOCK)
        s = jnp.where(kpos[None, :] <= qpos[:, None], s, -jnp.inf)
        p = jax.nn.softmax(s, axis=-1)
        return jnp.einsum('bhqk,bhkd->bhqd', p, vh)

    o = lax.map(block, (q_blocks, F_blocks, jnp.arange(nb)))
    return o.transpose(1, 0, 3, 2, 4).reshape(B, T, FOX_WIDTH).astype(q.dtype)

def first_inputs(seed: int = 0) -> dict:
    key = jax.random.key(seed)
    ks = jax.random.split(key, 16)
    f32 = jnp.float32
    nrm = lambda k, shape: jax.random.normal(k, shape, f32)
    return {
        "x": nrm(ks[0], (BATCH, SEQ, D_MODEL)),
        "ln1": 1.0 + 0.02 * nrm(ks[1], (DEPTH, D_MODEL)),
        "w_in": nrm(ks[2], (DEPTH, D_MODEL, IN_WIDTH)) * D_MODEL ** -0.5,
        "w_pool": nrm(ks[3], (DEPTH, POOL_GROUPS, POOL_GROUP, POOL_GROUP)) * POOL_GROUP ** -0.5,
        "pool_scale": 0.5 + 0.1 * nrm(ks[4], (DEPTH, POOL_WIDTH)),
        "w_a_up": nrm(ks[5], (DEPTH, GLA_GATE_RANK, GLA_WIDTH)) * GLA_GATE_RANK ** -0.5,
        "b_a": 0.1 * nrm(ks[6], (DEPTH, GLA_WIDTH)),
        "gla_gn": 1.0 + 0.02 * nrm(ks[7], (DEPTH, GLA_WIDTH)),
        "b_f": 3.0 + 0.5 * nrm(ks[8], (DEPTH, FOX_HEADS)),
        "w_o": nrm(ks[9], (DEPTH, D_MODEL, D_MODEL)) * D_MODEL ** -0.5,
        "ln2": 1.0 + 0.02 * nrm(ks[10], (DEPTH, D_MODEL)),
        "w_gu": nrm(ks[11], (DEPTH, D_MODEL, 2 * D_FF)) * D_MODEL ** -0.5,
        "w_down": nrm(ks[12], (DEPTH, D_FF, D_MODEL)) * D_FF ** -0.5,
        "ln_f": 1.0 + 0.02 * nrm(ks[13], (D_MODEL,)),
    }

def first_block(x, ln1, w_in, w_pool, pool_scale, w_a_up, b_a, gla_gn, b_f, w_o, ln2, w_gu, w_down, ln_f):
    pts = _split_points()
    for l in range(DEPTH):
        h = rmsnorm(x, ln1[l])
        z = jnp.einsum('btd,de->bte', h, w_in[l])
        u_pool, gq, gk, gv, gg, ga, fq, fk, fv, ff = jnp.split(z, pts, axis=-1)
        y_pool = pool_mixer(u_pool, w_pool[l], pool_scale[l])
        y_gla = gla_mixer(gq, gk, gv, gg, ga, w_a_up[l], b_a[l], gla_gn[l])
        y_fox = fox_mixer(fq, fk, fv, ff, b_f[l])
        mix = jnp.concatenate([y_pool.astype(x.dtype), y_gla.astype(x.dtype), y_fox.astype(x.dtype)], axis=-1)
        x = x + jnp.einsum('btd,de->bte', mix, w_o[l])
        h = rmsnorm(x, ln2[l])
        gate, up = jnp.split(jnp.einsum('btd,df->btf', h, w_gu[l]), 2, axis=-1)
        x = x + jnp.einsum('btf,fd->btd', jax.nn.silu(gate) * up, w_down[l])
    return rmsnorm(x, ln_f)


MLA_HEADS = 8
MLA_NOPE = 64
MLA_ROPE = 32
MLA_V = 64
MLA_Q_RANK = 384
MLA_KV_RANK = 256
ROPE_BASE = 10000.0
MLA_WIDTH = MLA_HEADS * MLA_V
DSA_HEADS = 8
DSA_HEAD_DIM = 64
DSA_WIDTH = DSA_HEADS * DSA_HEAD_DIM
IDX_HEADS = 8
IDX_DIM = 32
TOPK_MAX = 256
REL_BUCKETS = 32
REL_MAX_DIST = 128

IN_SPLITS = (MLA_Q_RANK, MLA_KV_RANK, MLA_ROPE, MLA_WIDTH,
             DSA_WIDTH, DSA_WIDTH, DSA_WIDTH, DSA_WIDTH,
             IDX_HEADS * IDX_DIM, IDX_DIM, IDX_HEADS,
             D_MODEL, D_MODEL)
IN_TOTAL = sum(IN_SPLITS)


def rmsnorm_2(x, g):
    xf = x.astype(jnp.float32)
    y = xf * lax.rsqrt(jnp.mean(xf * xf, axis=-1, keepdims=True) + EPS)
    return (y * g.astype(jnp.float32)).astype(x.dtype)

def rope(x, pos):
    half = x.shape[-1] // 2
    freqs = ROPE_BASE ** (-jnp.arange(half, dtype=jnp.float32) / half)
    ang = pos.astype(jnp.float32)[:, None] * freqs[None, :]
    cos = jnp.cos(ang)[None, :, None, :].astype(x.dtype)
    sin = jnp.sin(ang)[None, :, None, :].astype(x.dtype)
    x1, x2 = x[..., :half], x[..., half:]
    return jnp.concatenate([x1 * cos - x2 * sin, x1 * sin + x2 * cos], axis=-1)

def t5_bucket(rel):
    nb = REL_BUCKETS // 2
    max_exact = nb // 2
    ret = (rel > 0).astype(jnp.int32) * nb
    n = jnp.abs(rel)
    nf = jnp.maximum(n, 1).astype(jnp.float32)
    large = max_exact + (jnp.log(nf / max_exact) / np.log(REL_MAX_DIST / max_exact)
                         * (nb - max_exact)).astype(jnp.int32)
    large = jnp.minimum(large, nb - 1)
    return ret + jnp.where(n < max_exact, n, large)

def to_blocks(a):
    return jnp.moveaxis(a.reshape((a.shape[0], -1, Q_BLOCK) + a.shape[2:]), 1, 0)

def from_blocks(a):
    a = jnp.moveaxis(a, 0, 1)
    return a.reshape((a.shape[0], -1) + a.shape[3:])

def mla_attention(q_nope, q_pe, k_nope, k_pe, v, pos):
    scale = (MLA_NOPE + MLA_ROPE) ** -0.5
    key_chunk = pos // CHUNK

    def block(args):
        qn, qp, qpos = args
        logits = (jnp.einsum('bqhd,bkhd->bhqk', qn, k_nope)
                  + jnp.einsum('bqhr,bkr->bhqk', qp, k_pe))
        logits = logits.astype(jnp.float32) * scale
        mask = key_chunk[None, :] <= (qpos // CHUNK)[:, None]
        logits = jnp.where(mask[None, None], logits, -jnp.inf)
        p = jax.nn.softmax(logits, axis=-1).astype(v.dtype)
        return jnp.einsum('bhqk,bkhd->bqhd', p, v)

    out = lax.map(block, (to_blocks(q_nope), to_blocks(q_pe), pos.reshape(-1, Q_BLOCK)))
    return from_blocks(out)

def dsa_attention(q, k, v, q_idx, k_idx, w_idx, rel_bias, pos, topk):
    scale = DSA_HEAD_DIM ** -0.5
    key_chunk = pos // CHUNK
    gather = jax.vmap(lambda src, ids: src[ids])

    def block(args):
        qb, qi, wi, qpos = args
        qchunk = qpos // CHUNK
        s = jnp.einsum('bqhd,bkd->bqhk', qi, k_idx).astype(jnp.float32) * (IDX_DIM ** -0.5)
        score = jnp.einsum('bqhk,bqh->bqk', jax.nn.relu(s),
                           wi.astype(jnp.float32) * (IDX_HEADS ** -0.5))
        admissible = key_chunk[None, :] <= qchunk[:, None]
        score = jnp.where(admissible[None], score, -jnp.inf)
        _, idx = lax.top_k(score, topk)
        valid = (idx // CHUNK) <= qchunk[None, :, None]
        k_sel = gather(k, idx)
        v_sel = gather(v, idx)
        logits = jnp.einsum('bqhd,bqkhd->bhqk', qb, k_sel).astype(jnp.float32) * scale
        bias = rel_bias[t5_bucket(idx - qpos[None, :, None])]
        logits = logits + jnp.transpose(bias, (0, 3, 1, 2)).astype(jnp.float32)
        logits = jnp.where(valid[:, None], logits, -jnp.inf)
        p = jax.nn.softmax(logits, axis=-1).astype(v.dtype)
        return jnp.einsum('bhqk,bqkhd->bqhd', p, v_sel)

    out = lax.map(block, (to_blocks(q), to_blocks(q_idx), to_blocks(w_idx),
                          pos.reshape(-1, Q_BLOCK)))
    return from_blocks(out)

def second_inputs(seed: int = 0) -> dict:
    key = jax.random.key(seed)
    ks = jax.random.split(key, 13)

    def dense(k, shape):
        return jax.random.normal(k, shape, jnp.float32) * shape[-2] ** -0.5

    def gain(k, shape):
        return 1.0 + 0.05 * jax.random.normal(k, shape, jnp.float32)

    return {
        'x': jax.random.normal(ks[0], (BATCH, SEQ, D_MODEL), jnp.float32),
        'norm_g': gain(ks[1], (DEPTH, D_MODEL)),
        'w_in': dense(ks[2], (DEPTH, D_MODEL, IN_TOTAL)),
        'g_q_lat': gain(ks[3], (DEPTH, MLA_Q_RANK)),
        'w_uq': dense(ks[4], (DEPTH, MLA_Q_RANK, MLA_HEADS * (MLA_NOPE + MLA_ROPE))),
        'g_kv_lat': gain(ks[5], (DEPTH, MLA_KV_RANK)),
        'w_ukv': dense(ks[6], (DEPTH, MLA_KV_RANK, MLA_HEADS * (MLA_NOPE + MLA_V))),
        'w_o_a': dense(ks[7], (DEPTH, MLA_WIDTH, D_MODEL)),
        'w_o_b': dense(ks[8], (DEPTH, DSA_WIDTH, D_MODEL)),
        'w_out': dense(ks[9], (DEPTH, D_MODEL, D_MODEL)),
        'rel_bias': 0.5 * jax.random.normal(ks[10], (REL_BUCKETS, DSA_HEADS), jnp.float32),
        'final_g': gain(ks[11], (D_MODEL,)),
    }

def second_block(x, norm_g, w_in, g_q_lat, w_uq, g_kv_lat, w_ukv, w_o_a, w_o_b, w_out,
              rel_bias, final_g):
    B, S, _ = x.shape
    pos = jnp.arange(S, dtype=jnp.int32)
    topk = min(TOPK_MAX, S // 4)
    cuts = np.cumsum(IN_SPLITS)[:-1].tolist()
    for l in range(DEPTH):
        h = rmsnorm_2(x, norm_g[l])
        (q_lat, c_kv, k_rope, z_a, q_b, k_b, v_b, z_b,
         q_idx, k_idx, w_idx, gate_a, gate_b) = jnp.split(h @ w_in[l], cuts, axis=-1)

        q = (rmsnorm_2(q_lat, g_q_lat[l]) @ w_uq[l]).reshape(B, S, MLA_HEADS, MLA_NOPE + MLA_ROPE)
        q_nope, q_pe = q[..., :MLA_NOPE], rope(q[..., MLA_NOPE:], pos)
        kv = (rmsnorm_2(c_kv, g_kv_lat[l]) @ w_ukv[l]).reshape(B, S, MLA_HEADS, MLA_NOPE + MLA_V)
        k_nope, v_a = kv[..., :MLA_NOPE], kv[..., MLA_NOPE:]
        k_pe = rope(k_rope[:, :, None, :], pos)[:, :, 0, :]
        y_a = mla_attention(q_nope, q_pe, k_nope, k_pe, v_a, pos).reshape(B, S, MLA_WIDTH)
        y_a = y_a * jax.nn.silu(z_a)

        y_b = dsa_attention(q_b.reshape(B, S, DSA_HEADS, DSA_HEAD_DIM),
                            k_b.reshape(B, S, DSA_HEADS, DSA_HEAD_DIM),
                            v_b.reshape(B, S, DSA_HEADS, DSA_HEAD_DIM),
                            q_idx.reshape(B, S, IDX_HEADS, IDX_DIM), k_idx, w_idx,
                            rel_bias, pos, topk).reshape(B, S, DSA_WIDTH)
        y_b = y_b * jax.nn.silu(z_b)

        merged = (jax.nn.sigmoid(gate_a) * (y_a @ w_o_a[l])
                  + jax.nn.sigmoid(gate_b) * (y_b @ w_o_b[l]))
        x = x + merged @ w_out[l]
    return rmsnorm_2(x, final_g)


def setup_inputs(seed=0):
    out = dict(first_inputs(seed))
    for name, value in second_inputs(seed + 1).items():
        if name != "x":
            out[name + "_2"] = value
    return out


def reference(
    x, ln1, w_in, w_pool, pool_scale, w_a_up, b_a, gla_gn, b_f, w_o, ln2, w_gu, w_down, ln_f,
    norm_g_2, w_in_2, g_q_lat_2, w_uq_2, g_kv_lat_2, w_ukv_2, w_o_a_2, w_o_b_2, w_out_2,
    rel_bias_2, final_g_2,
):
    x = first_block(
        x, ln1, w_in, w_pool, pool_scale, w_a_up, b_a, gla_gn, b_f, w_o, ln2, w_gu, w_down,
        ln_f,
    )
    return second_block(
        x, norm_g_2, w_in_2, g_q_lat_2, w_uq_2, g_kv_lat_2, w_ukv_2, w_o_a_2, w_o_b_2, w_out_2,
        rel_bias_2, final_g_2,
    )


_drawn_inputs = setup_inputs


def setup_inputs(seed=0):
    import zlib

    import numpy as np

    out = dict(_drawn_inputs(seed))
    spreads = {}
    factors = {'ln1': 3.177,
     'b_a': 3.667,
     'gla_gn': 7.651,
     'ln2': 3.874,
     'norm_g_2': 4.293,
     'g_q_lat_2': 8.0,
     'g_kv_lat_2': 8.0}
    for name, (base, spread) in spreads.items():
        noise = np.random.default_rng([zlib.crc32(name.encode()), seed]).standard_normal(out[name].shape)
        drawn = base * np.exp(spread * noise) if base else spread * noise
        out[name] = __import__('jax').numpy.asarray(drawn.astype(out[name].dtype))
    for name, factor in factors.items():
        out[name] = (out[name] * factor).astype(out[name].dtype)
    return out
```

```python
from contextlib import ExitStack

import numpy as np

import concourse.bass as bass
from concourse import mybir
from concourse.alu_op_type import AluOpType as ALU

F32 = mybir.dt.float32
F32R = mybir.dt.float32r
BF16 = mybir.dt.bfloat16
ACT = mybir.ActivationFunctionType
AX = mybir.AxisListType.X

D = 1024
T = 512
NK = D // 128
DFF = 2816
FH = DFF // 2 // 128
EPS = 1e-6
UT = 8
NTILES = 1312
BIG = 1.0e30
GONE = -3.0e38
REL = 640

O_POOL, O_GQ, O_GK, O_GV, O_GG, O_GA = 0, 256, 512, 768, 1024, 1280
O_FQ, O_FK, O_FV, O_FF = 1296, 1808, 2320, 2832
P_QL, P_CKV, P_KR, P_ZA = 0, 384, 640, 672
P_QB, P_KB, P_VB, P_ZB = 1184, 1696, 2208, 2720
P_QI, P_KI, P_WI, P_GA, P_GB = 3232, 3488, 3520, 3528, 4552

VEC = {}
_at = 0
for _name, _n in (("ln1", 8), ("ln2", 8), ("ln_f", 8), ("norm_g_2", 8), ("final_g_2", 8),
                  ("pool_scale", 2), ("b_a", 2), ("gla_gn", 2), ("g_q_lat_2", 3),
                  ("g_kv_lat_2", 2), ("b_f", 1)):
    VEC[_name] = (_at, _n)
    _at += _n
NVEC = _at


def flat(tokens):
    out = []
    for t in tokens:
        if t is None:
            continue
        if isinstance(t, list):
            out += flat(t)
        else:
            out.append(t)
    return out


class Line:

    def __init__(self, sem, alone=False):
        self.sem, self.n, self.todo, self.seen, self.alone = sem, 0, [], {}, alone

    def waits(self, after):
        need = []
        for sem, value in flat(after):
            if self.seen.get(id(sem), 0) < value:
                self.seen[id(sem)] = value
                need.append((sem, value))
        return need

    def __call__(self, make, *after, tell=True):
        if self.alone and self.n:
            after = (*after, (self.sem, self.n))
        self.todo.append((self.waits(after), make, (self.sem, 1) if tell else None))
        if tell:
            self.n += 1
            return (self.sem, self.n)
        return None

    def dma(self, landing, make, *after):
        self.todo.append((self.waits(after), make, (landing.sem, 16)))
        landing.n += 16
        return (landing.sem, landing.n)

    def emit(self, eng):
        for need, make, tell in self.todo:
            for sem, value in need:
                eng.wait_ge(sem, value)
            ins = make(eng)
            if tell:
                ins.then_inc(*tell)


class Landing:

    def __init__(self, sem):
        self.sem, self.n = sem, 0


class Slot:
    def __init__(self, ring, i, free):
        self.ring, self.i, self.buf, self.free = ring, i, ring.bufs[i], free

    def release(self, *tokens):
        self.ring.free[self.i] = flat(tokens)


class Ring:

    def __init__(self, bufs, free=()):
        self.bufs, self.free, self.n = bufs, [list(free) for _ in bufs], 0

    def take(self):
        i = self.n % len(self.bufs)
        self.n += 1
        free = self.free[i]
        assert free is not None, "a buffer is taken before it was released"
        self.free[i] = None
        return Slot(self, i, free)


def taken(ring, count=1):
    while any(ring.free[(ring.n + i) % len(ring.bufs)] is None for i in range(count)):
        yield "not yet"
    return [ring.take() for _ in range(count)]


def weave(main, side, per):
    due = 0.0
    live = True
    rates = per if isinstance(per, list) else [per]
    for n, _ in enumerate(main):
        due += rates[min(n, len(rates) - 1)]
        while live and due >= 1:
            due -= 1
            got = next(side, "end")
            live = got != "end"
            if got == "not yet":
                due = 0.0
    for _ in side:
        pass


def build(nc, wall, xT, vecs, wa, wp, relb, cf, cph, coh, cb, scratch, outT):
    plan = []
    ctx = ExitStack()
    with ctx:
        KB = 1024
        base = 16896
        place = {"at": base}

        def at(name, shape, dt, off):
            return nc.alloc_sbuf_tensor_at(name, shape, dt, offset=off)

        def fixed(name, shape, dt=F32):
            size = int(np.prod(shape[1:])) * (2 if dt == BF16 else 4)
            size = (size + 31) // 32 * 32
            t = at(name, shape, dt, place["at"])
            place["at"] += size
            return t

        def sem(name):
            return ctx.enter_context(nc.semaphore(name))

        X = fixed("X", [128, NK, T])
        HH = fixed("HH", [128, NK, T], F32R)
        HL = fixed("HL", [128, NK, T], F32R)
        NST, NW = 3, 4
        WS = fixed("WS", [128, NST, UT * 128])
        WH = fixed("WH", [128, NW, UT * 128], F32R)
        WL = fixed("WL", [128, NW, UT * 128], F32R)
        ident = fixed("ident", [128, 128])
        RT = fixed("RT", [128, T])
        identb = fixed("identb", [128, 3, 128], BF16)
        ones = fixed("ones", [128, 128])
        V = fixed("V", [128, NVEC])
        eps = fixed("eps", [128, 1])
        Rb = fixed("Rb", [128, T])
        Rf_at = place["at"]
        Rf = fixed("Rf", [128, T])
        rtok = fixed("rtok", [128, 16])
        acc0 = fixed("acc0", [128, T])
        acc1_at = place["at"]
        acc = [acc0, fixed("acc1", [128, T])]
        sqb = [fixed("sq0", [128, T]), fixed("sq1", [128, T])]
        tmpb = [fixed("tmp0", [128, T]), fixed("tmp1", [128, T])]
        small = fixed("small", [128, 32])
        wi = fixed("wi", [128, 4, 8])
        m8 = fixed("m8", [128, 8])
        rbs = fixed("rbs", [32, 8])
        wa_sb = nc.alloc_sbuf_tensor_at("wa_sb", [16, 256], F32, offset=Rf_at)
        wp_sb = nc.alloc_sbuf_tensor_at("wp_sb", [128, 2, 128], F32, offset=Rf_at + KB)
        gmask = nc.alloc_sbuf_tensor_at("gmask", [128, 128], F32, offset=acc1_at)
        gones = nc.alloc_sbuf_tensor_at("gones", [128, 128], F32, offset=acc1_at + 512)
        R = place["at"]
        assert R + 92 * KB <= 229368, R + 92 * KB - 229368

        def sub(name, shape, dt, off):
            return at(name, shape, dt, R + int(off * KB))

        MH = sub("MH", [128, 8, T], F32R, 0)
        ML = sub("ML", [128, 8, T], F32R, 16)
        g_bc0 = sub("g_bc", [128, T], F32, 8)
        g_e = sub("g_e", [128, T], F32, 10)
        g_qi = sub("g_qi", [128, T], F32, 12)
        g_ki = sub("g_ki", [128, T], F32, 14)
        g_qe = sub("g_qe", [128, T], F32, 24)
        g_kh = sub("g_kh", [128, T], F32, 26)
        g_kt = sub("g_kt", [128, 4, 128], F32, 28)
        g_b2 = sub("g_b2", [128, T], F32, 30)
        g_q = sub("g_q", [128, 2, T], F32, 32)
        g_k = sub("g_k", [128, 2, T], F32, 36)
        g_g = sub("g_g", [128, 2, T], F32, 40)
        g_v = sub("g_v", [128, 4, 256], F32, 44)
        f_qk = [sub(f"f_qk{i}", [128, 2, T], F32, 48 + 4 * i) for i in range(2)]
        f_v = sub("f_v", [128, 4, T], F32, 56)
        f_lq = sub("f_lq", [128, 2, T], BF16, 64)
        f_lk = sub("f_lk", [128, 2, T], BF16, 66)
        Pb = [sub(f"Pb{i}", [128, T], F32, 68 + 2 * i) for i in range(2)]
        PTb = [sub(f"PTb{i}", [128, T], F32, 72 + 2 * i) for i in range(2)]
        g_S = sub("g_S", [128, 8, 128], F32, 76)
        g_at = sub("g_at", [128, 2, 4, 128], F32, 80)
        icnt = sub("icnt", [128, 2, T], F32, 84)
        rset = sub("rset", [128, T], F32, 88)
        p_u = sub("p_u", [128, 2, 16 + T], F32, 48)
        p_a = [sub(f"p_a{i}", [128, 2, 16 + T], F32, 52.25 + 4.25 * i) for i in range(2)]
        smz = sub("smz", [128, T], F32, 90)
        GH = sub("GH", [128, FH, T], F32R, 0)
        GL = sub("GL", [128, FH, T], F32R, 22)
        fg = [sub(f"fg{i}", [128, T], F32, 44 + 2 * i) for i in range(3)]
        fs = [sub(f"fs{i}", [128, T], F32, 50 + 2 * i) for i in range(3)]
        fa = [sub(f"fa{i}", [128, T], F32, 56 + 2 * i) for i in range(3)]
        i_q = sub("i_q", [128, 2, T], F32, 0)
        i_s = sub("i_s", [128, T], F32, 4)
        i_k = sub("i_k", [128, T], F32, 6)
        score = sub("score", [128, 1152], F32, 8)
        nmask = sub("nmask", [128, 1152], BF16, 12.75)
        flip = sub("flip", [128, 128], F32, 15.25)
        LQH = sub("LQH", [128, 3, T], F32R, 16)
        LQL = sub("LQL", [128, 3, T], F32R, 22)
        LKH = sub("LKH", [128, 2, T], F32R, 28)
        LKL = sub("LKL", [128, 2, T], F32R, 32)
        b_qk = [sub(f"b_qk{i}", [128, 2, T], F32, 16 + 4 * i) for i in range(2)]
        b_v = sub("b_v", [128, 4, T], F32, 24)
        b_t = [sub(f"b_t{i}", [128, T], F32, 32 + 2 * i) for i in range(2)]
        YAH = sub("YAH", [128, 4, T], F32R, 36)
        YAL = sub("YAL", [128, 4, T], F32R, 44)
        a_q = [sub(f"a_q{i}", [128, T], F32, 52 + 4 * i) for i in range(4)]
        a_k = [sub(f"a_k{i}", [128, T], F32, 54 + 4 * i) for i in range(4)]
        a_v = sub("a_v", [128, 4, T], F32, 68)
        YBH = sub("YBH", [128, 4, T], F32R, 52)
        YBL = sub("YBL", [128, 4, T], F32R, 60)
        zb = [sub(f"zb{i}", [128, T], F32, 76 + 2 * i) for i in range(2)]
        Pc = [sub(f"Pc{i}", [128, T], F32, 80 + 2 * i) for i in range(2)]
        PTc = [sub(f"PTc{i}", [128, T], F32, 84 + 2 * i) for i in range(2)]
        RQ = sub("RQ", [128, T], F32, 88)
        RK = sub("RK", [128, T], F32, 90)
        oh = sub("oh", [32, REL], F32, 16)
        brow = sub("brow", [8, REL], F32, 19)
        MGH = sub("MGH", [128, 8, T], F32R, 0)
        MGL = sub("MGL", [128, 8, T], F32R, 16)

        bank = [ctx.enter_context(nc.psum_tensor(f"bank{i}", [128, 512], F32)) for i in range(8)]

        s_pe, s_act, s_dve, s_pool, s_sp = (sem(n) for n in ("pe", "act", "dve", "pool", "sp"))
        PE, AC, DV, PO, SP = Line(s_pe), Line(s_act), Line(s_dve), Line(s_pool, alone=True), Line(s_sp)
        stage_in = [Landing(sem(f"w_in{i}")) for i in range(NST)]
        nland = [0]

        def landing():
            nland[0] += 1
            return Landing(sem(f"land{nland[0]}"))

        dense_ring = Ring(bank[0:2])
        s_ring = Ring(bank[2:4])
        t_ring = Ring(bank[4:6])
        y_ring = Ring(bank[6:8])
        sq_ring = Ring(sqb)
        tmp_ring = Ring(tmpb)

        def mm(out, l, r, start, stop, *after, tell=False):
            return PE(lambda e: nc.tensor.matmul(out, l, r, start=start, stop=stop), *after, tell=tell)

        def act(out, in_, f, *after, bias=None, scale=None, acc=None):
            kw = {}
            if bias is not None:
                kw["bias"] = bias
            if scale is not None:
                kw["scale"] = scale
            if acc is not None:
                kw["accum_out"] = acc
            return AC(lambda e: nc.scalar.activation(out, in_, f, **kw), *after)

        def tt(line, out, a, b, op, *after):
            return line(lambda e: e.tensor_tensor(out, a, b, op), *after)

        def ts(line, out, a, s1, s2, op0, op1, *after):
            if op1 is None:
                return line(lambda e: e.tensor_scalar(out, a, s1, None, op0), *after)
            return line(lambda e: e.tensor_scalar(out, a, s1, s2, op0, op1), *after)

        def stt(line, out, a, s, b, op0, op1, *after):
            return line(lambda e: e.scalar_tensor_tensor(out, a, s, b, op0, op1), *after)

        def vec(name, c):
            return V[:, VEC[name][0] + c:VEC[name][0] + c + 1]

        def f32(ap):
            return ap.bitcast(F32)

        NU = NTILES // UT
        wst = {"ready": {}, "free": [None] * NW, "conv": 0, "dma": 0, "stage_free": [None] * NST,
               "landed": {}}

        def load_unit():
            u = wst["dma"]
            if u >= NU:
                return
            wst["dma"] += 1
            k = u % NST
            wst["landed"][u] = SP.dma(stage_in[k], lambda e: e.dma_start(WS[:, k, :], wall[u]),
                                      wst["stage_free"][k])

        def split_unit():
            u = wst["conv"]
            if u >= NU:
                return
            wst["conv"] += 1
            k, j = u % NST, u % NW
            a = act(WH[:, j, :], WS[:, k, :], ACT.Copy, wst["landed"][u], wst["free"][j])
            d = tt(DV, WL[:, j, :], WS[:, k, :], f32(WH[:, j, :]), ALU.subtract, a)
            wst["free"][j] = "busy"
            wst["ready"][u] = d
            wst["stage_free"][k] = [d, wst["landed"][u]]
            load_unit()

        tile_no = [0]
        behind = {"gens": [], "due": 0.0, "per": 0.0}

        def go_behind():
            behind["due"] += behind["per"]
            while behind["due"] >= 1 and behind["gens"]:
                behind["due"] -= 1
                if next(behind["gens"][0], "end") == "end":
                    behind["gens"].pop(0)

        def next_tile(what):
            t = tile_no[0]
            tile_no[0] += 1
            plan.append(what)
            u = t // UT
            while wst["conv"] <= min(u + 2, NU - 1):
                split_unit()
            c = (t % UT) * 128
            j = u % NW
            return WH[:, j, c:c + 128], WL[:, j, c:c + 128], wst["ready"][u], t

        def tile_done(t, tok):
            if t % UT == UT - 1:
                wst["free"][(t // UT) % NW] = tok

        def cols(c0, n=128):
            return tuple(range(c0, c0 + n))

        def dense(mat, k0, column, rhs, done, steps=2, ring=None, later=None):
            slot = (ring or dense_ring).take()
            n = len(rhs)
            for k in range(n):
                while rhs[k] is None:
                    yield "not yet"
                rh, rl, tok = rhs[k]
                wh, wl, ready, t = next_tile((mat, k0 + k, column))
                first, last = k == 0, k == n - 1
                end = last or t % UT == UT - 1
                mm(slot.buf[:, :], wh, rh, first, False, slot.free if first else None, ready, tok)
                mm(slot.buf[:, :], wh, rl, False, False)
                tok2 = mm(slot.buf[:, :], wl, rh, False, last, tell=end)
                if end:
                    wst["last_pe"] = tok2
                    tile_done(t, tok2)
                if k % steps == steps - 1 and not last:
                    go_behind()
                    yield
            if later is None:
                slot.release(done(slot.buf, tok2))
            else:
                later.append(lambda: slot.release(done(slot.buf, tok2)))
            yield

        def dense_tok(mat, ks, column, lhs, done):
            while tile_no[0] % 2:
                _, _, _, t = next_tile((None, 0, ()))
                tile_done(t, wst["last_pe"])
            tiles, starts = [], []
            for k in ks:
                a = next_tile((mat, k, column[:128]))
                b = next_tile((mat, k, column[128:]))
                starts.append(a[3])
                j, c = (a[3] // UT) % NW, (a[3] % UT) * 128
                tiles.append((WH[:, j, c:c + 256], WL[:, j, c:c + 256], a[2]))
            for tb in range(4):
                slot = dense_ring.take()
                cs = slice(tb * 128, tb * 128 + 128)
                for k, (wh, wl, ready) in enumerate(tiles):
                    hh, hl, tok = lhs[k]
                    first, last = k == 0, k == len(tiles) - 1
                    mm(slot.buf[:, 0:256], hh[:, cs], wh, first, False, slot.free if first else None,
                       ready, tok)
                    mm(slot.buf[:, 0:256], hh[:, cs], wl, False, False)
                    tok2 = mm(slot.buf[:, 0:256], hl[:, cs], wh, False, last, tell=last)
                    if k % 4 == 3 and not last:
                        go_behind()
                        yield
                slot.release(done(slot.buf, tb, tok2))
                if tb == 3:
                    wst["last_pe"] = tok2
                    for a in starts:
                        tile_done(a, tok2)
                        tile_done(a + 1, tok2)
                yield

        def split_act(hi, lo, src, g, *after, extra=None):
            if g is None:
                a = act(hi, src, ACT.Copy, *after)
                d = tt(DV, lo, src, f32(hi), ALU.subtract, a, *after)
            else:
                a = act(hi, src, ACT.Copy, *after, scale=g)
                d = stt(DV, lo, src, g, f32(hi), ALU.mult, ALU.subtract, a, *after)
            return d

        class Sum:
            def __init__(self, buf, free):
                self.buf, self.tok, self.free = buf, None, free

            def add(self, src, scale, *after, line=None):
                line = line or PO
                s = sq_ring.take()
                a = act(s.buf[:, :], src, ACT.Square, *after, s.free, scale=scale)
                if self.tok is None:
                    self.tok = line(lambda e: e.tensor_copy(self.buf[:, :], s.buf[:, :]), a, self.free)
                else:
                    self.tok = tt(line, self.buf[:, :], self.buf[:, :], s.buf[:, :], ALU.add, a, self.tok)
                s.release(self.tok)
                return a

        def total(sum_):
            slot = t_ring.take()
            tok = mm(slot.buf[:, :], ones[:, :], sum_.buf[:, :], True, True, sum_.tok, slot.free,
                     c_ones, tell=True)
            return slot, tok

        def total_tok(sums):
            slot = t_ring.take()
            for i, s in enumerate(sums):
                for tb in range(4):
                    last = i == len(sums) - 1 and tb == 3
                    tok = mm(slot.buf[:, 4 * i + tb:4 * i + tb + 1], s.buf[:, tb * 128:tb * 128 + 128],
                             ones[:, 0:1], True, True, s.tok, slot.free, c_ones, tell=last)
            return slot, tok

        def rsqrt(dst, src, n, *after):
            a = act(dst, src, ACT.Ln, *after, scale=1.0 / n, bias=eps[:, :])
            return a, act(dst, dst, ACT.Exp, a, scale=-0.5)

        c_ones = PO(lambda e: e.memset(ones[:, :], 1.0))
        c_eps = PO(lambda e: e.memset(eps[:, :], EPS))
        vtok = SP.dma(landing(), lambda e: e.dma_start(V[:, :], vecs))
        x_in = []
        for c in range(NK):
            x_in.append(SP.dma(landing(), lambda e, c=c: e.dma_start(X[:, c, :], xT[:, c, :])))
            if c in (1, 3, 6):
                load_unit()
        lc = landing()
        SP.dma(lc, lambda e: e.dma_start(ident[:, :], cf[:, 0:128]))
        SP.dma(lc, lambda e: e.dma_start(RT[:, :], cf[:, 128:640]))
        SP.dma(lc, lambda e: e.dma_start(identb[:, :, :], cb))
        SP.dma(lc, lambda e: e.dma_start(gmask[:, :], cf[:, 640:768]))
        SP.dma(lc, lambda e: e.dma_start(gones[:, :], cf[:, 768:896]))
        SP.dma(lc, lambda e: e.dma_start(wa_sb[:, :], wa))
        SP.dma(lc, lambda e: e.dma_start(wp_sb[:, :, :], wp))
        SP.dma(lc, lambda e: e.dma_start(icnt[:, :, :], cph[:, 0:1024].rearrange("p (a n) -> p a n", a=2)))
        consts = SP.dma(lc, lambda e: e.dma_start(rset[:, :], cph[:, 1024:1536]))

        sx = Sum(acc[0], None)
        h = []
        for c in range(NK):
            d = split_act(HH[:, c, :], HL[:, c, :], X[:, c, :], vec("ln1", c), x_in[c], vtok)
            h.append((HH[:, c, :], HL[:, c, :], d))
            if c in (1, 5):
                split_unit()
        for c in range(NK):
            sx.add(X[:, c, :], None, x_in[c], line=DV)

        stat = {}

        def norm1():
            s1, k1 = total(sx)
            s2, k2 = total_tok([sx])
            a1 = act(Rb[:, :], s1.buf[:, :], ACT.Ln, k1, c_eps, scale=1.0 / D, bias=eps[:, :])
            stat["c"] = act(rtok[:, 0:4], s2.buf[:, 0:4], ACT.Ln, k2, scale=1.0 / D, bias=eps[:, :])
            s1.release(a1)
            s2.release(stat["c"])
            stat["b"] = act(Rb[:, :], Rb[:, :], ACT.Exp, a1, scale=-0.5)
            stat["t"] = act(rtok[:, 0:4], rtok[:, 0:4], ACT.Exp, stat["c"], scale=-0.5)

        def run(gen):
            for _ in gen:
                pass

        def out_scaled(dst, k):
            def done(b, tok):
                d = stt(DV, dst, b[:, :], float(k), Rb[:, :], ALU.mult, ALU.mult, tok, stat["b"])
                out_tok.append(d)
                return d
            return done

        out_tok = []

        def last_out():
            return out_tok[-1]

        early = Ring([bank[0], bank[1], bank[6], bank[7]])
        waiting = []
        run(dense("w_in", 0, cols(O_GA, 16) + (-1,) * 16 + cols(O_FF, 8) + (-1,) * 88, h,
                  out_scaled(smz[:, :], 1.0), ring=early, later=waiting))
        run(dense("w_in", 0, cols(O_POOL), h, out_scaled(p_u[:, 0, 16:16 + T], 1.0), ring=early, later=waiting))
        gen = dense("w_in", 0, cols(O_POOL + 128), h, out_scaled(p_u[:, 1, 16:16 + T], 1.0), ring=early,
                    later=waiting)
        next(gen)
        norm1()
        run(gen)
        run(dense("w_in", 0, cols(O_GK), h, out_scaled(g_k[:, 0, :], 1.0), ring=early, later=waiting))
        for finish in waiting:
            finish()
        dense_ring.free = early.free[0:2]
        y_ring.free = early.free[2:4]
        sm_tok, pu_tok, tok_gk0 = out_tok[0], out_tok[1:3], out_tok[3]

        fr = slice(32, 40)
        zf = smz[fr, :]
        q1, q2 = tmp_ring.take(), sq_ring.take()
        w1, w2 = q1.buf[fr, :], q2.buf[fr, :]
        bf = V[fr, VEC["b_f"][0]:VEC["b_f"][0] + 1]
        d1 = act(w1, zf, ACT.Abs, sm_tok, q1.free, vtok, bias=bf)
        a1 = act(w1, w1, ACT.Exp, d1, scale=-1.0)
        a1 = act(w1, w1, ACT.Ln, a1, bias=1.0)
        d2 = ts(DV, w2, zf, bf, 0.0, ALU.add, ALU.min, sm_tok, q2.free)
        d2 = tt(DV, w2, w2, w1, ALU.subtract, d2, a1)
        F = sub("F", [128, T], F32, 72)
        parts = [sub(f"part{j}", [128, T], BF16, 16 + j) for j in range(3)]
        negs = [sub(f"neg{j}", [128, T], BF16, 19 + j) for j in range(3)]
        one = PO(lambda e: e.memset(w1, 1.0), d2)
        dF = DV(lambda e: e.tensor_tensor_scan(F[fr, :], w1, w2, 0.0, ALU.mult, ALU.add), one, d2)
        q1.release(dF)
        m1 = PO(lambda e: e.memset(f_lq[:, :, :], 1.0))
        m2 = PO(lambda e: e.memset(f_lk[:, :, :], 1.0))
        lF = landing()
        tokF = dF
        for j in range(3):
            part, neg = parts[j], negs[j]
            dp = DV(lambda e, part=part: e.tensor_copy(part[fr, :], F[fr, :]), tokF)
            dn = ts(DV, neg[fr, :], part[fr, :], -1.0, None, ALU.mult, None, dp)
            if j < 2:
                tokF = tt(DV, F[fr, :], F[fr, :], part[fr, :], ALU.subtract, dp)
            for src, dst, row, mk in ((part, f_lq, 3 + j, m1), (neg, f_lk, j, m2)):
                for hh in range(2):
                    f_aug = SP.dma(lF, lambda e, src=src, dst=dst, row=row, hh=hh: e.dma_start(
                        dst[row:row + 97:32, hh, :], src[32 + 4 * hh:36 + 4 * hh, :]), dp, dn, mk)
        q2.release(tokF, dF)

        def gla_front(hp):
            gb = (g_bc0, g_b2)[hp]
            t1, t2 = tmp_ring.take(), sq_ring.take()
            slot = t_ring.take()
            tok = mm(slot.buf[:, :], wa_sb[0:16, hp * 128:hp * 128 + 128], smz[0:16, :], True, True,
                     sm_tok, consts, slot.free, tell=True)
            d1 = act(t1.buf[:, :], slot.buf[:, :], ACT.Abs, tok, t1.free, vtok, bias=vec("b_a", hp))
            d2 = ts(DV, t2.buf[:, :], slot.buf[:, :], vec("b_a", hp), 0.0, ALU.add, ALU.min, d1, t2.free)
            slot.release(d2)
            a = act(t1.buf[:, :], t1.buf[:, :], ACT.Exp, d1, scale=-1.0)
            a = act(t1.buf[:, :], t1.buf[:, :], ACT.Ln, a, bias=1.0)
            d = tt(DV, t2.buf[:, :], t2.buf[:, :], t1.buf[:, :], ALU.subtract, d2, a)
            t1.release(d)
            g_last["bc", hp] = DV(lambda e: e.tensor_tensor_scan(gb[:, :], rset[:, :], t2.buf[:, :], 0.0,
                                                                 ALU.mult, ALU.add), d, consts)
            t2.release(g_last["bc", hp])

        def gla_pair(hp):
            g_bc, w, dbc = (g_bc0, g_b2)[hp], g_last.get("done"), g_last["bc", hp]
            bc = g_bc[:, :].rearrange("p (n c) -> p n c", c=64)
            e3 = g_e[:, :].rearrange("p (n c) -> p n c", c=64)
            ref = bc[:, :, 31:32].broadcast_to([128, 8, 64])
            lst = bc[:, :, 63:64].broadcast_to([128, 8, 64])
            t3 = tmp_ring.take()
            v3 = t3.buf[:, :].rearrange("p (n c) -> p n c", c=64)
            d = tt(DV, v3, bc, ref, ALU.subtract, dbc, t3.free)
            a = act(g_e[:, :], t3.buf[:, :], ACT.Exp, d, w, scale=1.0 / 16)
            q = g_q[:, hp, :]
            k = g_k[:, hp, :]
            dq = tt(DV, g_qi[:, :], q, g_e[:, :], ALU.mult, a, tok_gq[hp], w)
            a = act(g_e[:, :], t3.buf[:, :], ACT.Exp, dq, scale=-1.0 / 16)
            dk = tt(DV, g_ki[:, :], k, g_e[:, :], ALU.mult, a, tok_gk[hp])
            t3.release(a)
            a = act(g_e[:, :], g_bc[:, :], ACT.Exp, dk, dbc, scale=1.0 / 16)
            dqe = tt(DV, g_qe[:, :], q, g_e[:, :], ALU.mult, a)
            t4 = tmp_ring.take()
            v4 = t4.buf[:, :].rearrange("p (n c) -> p n c", c=64)
            d = tt(DV, v4, lst, bc, ALU.subtract, dbc, t4.free)
            a4 = act(t4.buf[:, :], t4.buf[:, :], ACT.Exp, d, scale=1.0 / 16)
            dkh = tt(DV, g_kh[:, :], k, t4.buf[:, :], ALU.mult, a4)
            t4.release(dkh)
            yield
            yield
            yield
            slot = t_ring.take()
            for tb in range(4):
                tok = PE(lambda e, tb=tb, b=slot.buf: nc.tensor.transpose(
                    b[:, tb * 128:tb * 128 + 128], g_kh[:, tb * 128:tb * 128 + 128], ident[:, :]),
                    dkh, slot.free, consts, tell=tb == 3)
            akt = act(g_kt[:, :, :].rearrange("p a n -> p (a n)"), slot.buf[:, :], ACT.Copy, tok)
            slot.release(akt)
            yield
            datt = []
            for hl in range(2):
                slot = s_ring.take()
                for n in range(8):
                    r = slice(64 * hl, 64 * hl + 64)
                    o = slice(64 * (n % 2), 64 * (n % 2) + 64)
                    tok = mm(slot.buf[o, 64 * (n // 2):64 * (n // 2) + 64], g_ki[r, 64 * n:64 * n + 64],
                             g_qi[r, 64 * n:64 * n + 64], True, True, dk, dq, slot.free, tell=n == 7)
                slot.tok = tok
                for par in range(2):
                    o = slice(64 * par, 64 * par + 64)
                    src = slot.buf[o, 0:256].rearrange("p (n c) -> p n c", c=64)
                    dst = g_at[o, hl, :, 64 * par:64 * par + 64]
                    hi = gmask[o, 0:64].unsqueeze(1).broadcast_to([64, 4, 64])
                    lo = gmask[o, 64:128].unsqueeze(1).broadcast_to([64, 4, 64])
                    x1 = tt(DV, dst, src, hi, ALU.min, slot.tok, consts, g_zero)
                    datt.append(tt(DV, dst, dst, lo, ALU.max, x1))
                slot.release(x1)
                yield
            kv = []
            for par in range(2):
                slot = s_ring.take()
                kv.append(slot)
                r = slice(64 * par, 64 * par + 64)
                for n4 in range(4):
                    tok = mm(slot.buf[:, n4 * 128:n4 * 128 + 128], g_kt[r, n4, :],
                             g_v[r, n4, hp * 128:hp * 128 + 128], True, True, akt, tok_gv, slot.free,
                             tell=n4 == 3)
                slot.tok = tok
            dS = g_zero
            first = [w, dbc]
            for n in range(7):
                slot = kv[n % 2]
                nd = []
                for hl in range(2):
                    r = slice(64 * hl, 64 * hl + 64)
                    src = slot.buf[r, (n // 2) * 128 + 64 * hl:(n // 2) * 128 + 64 * hl + 64]
                    nd.append(stt(DV, g_S[r, n + 1, 64 * hl:64 * hl + 64], g_S[r, n, 64 * hl:64 * hl + 64],
                                  g_e[r, 64 * n + 63:64 * n + 64], src, ALU.mult, ALU.add, slot.tok, dS,
                                  dqe, first))
                dS = nd[-1]
            kv[0].release(dS)
            kv[1].release(dS)
            yield
            yield
            slot = y_ring.take()
            for n4 in range(4):
                cs = slice(n4 * 128, n4 * 128 + 128)
                for hl in range(2):
                    mm(slot.buf[64 * hl:64 * hl + 64, cs], g_v[:, n4, (2 * hp + hl) * 64:(2 * hp + hl) * 64 + 64],
                       g_at[:, hl, n4, :], True, False, datt, slot.free, tok_gv)
                for par in range(2):
                    n = 2 * n4 + par
                    tok = mm(slot.buf[:, 64 * n:64 * n + 64], g_S[:, n, :], g_qe[:, 64 * n:64 * n + 64],
                             False, par == 1, dS, dqe, tell=True)
            sq = sq_ring.take()
            a = act(sq.buf[:, :], slot.buf[:, :], ACT.Square, tok, sq.free)
            o = g_q[:, hp, :]
            do = ts(DV, o, slot.buf[:, :], vec("gla_gn", hp), None, ALU.mult, None, a, tok)
            slot.release(do)
            ts_ = t_ring.take()
            tok = mm(ts_.buf[:, :], gones[:, :], sq.buf[:, :], True, True, a, ts_.free, g_ones, tell=True)
            t5 = tmp_ring.take()
            a, b = rsqrt(t5.buf[:, :], ts_.buf[:, :], 64, tok, t5.free)
            ts_.release(a)
            sq.release(tok)
            d = tt(DV, o, o, t5.buf[:, :], ALU.mult, b, do)
            t5.release(d)
            g_last["done"] = [d]
            g_last[hp] = d
            yield

        def gla_out():
            for hp in range(2):
                o = g_q[:, hp, :]
                d = tt(DV, o, o, g_g[:, hp, :], ALU.mult, g_last[hp], tok_gg[hp])
                e = split_act(MH[:, 2 + hp, :], ML[:, 2 + hp, :], o, None, d, f_aug)
                mix[2 + hp] = (MH[:, 2 + hp, :], ML[:, 2 + hp, :], e)
            yield

        g_ones = consts
        z1 = PO(lambda e: e.memset(g_S[:, :, :], 0.0))
        z2 = PO(lambda e: e.memset(g_at[:, :, :, :], 0.0))
        g_zero = [z1, z2]
        g_last = {}
        mix = [None] * 8
        tok_gq, tok_gk, tok_gg, tok_gv = [None] * 2, [tok_gk0, None], [None] * 2, []

        def silu_in_place(z, tok, ring):
            t = ring.take()
            a = act(t.buf[:, :], z, ACT.Tanh, tok, t.free)
            d = stt(DV, z, t.buf[:, :], 1.0, z, ALU.add, ALU.mult, a)
            t.release(d)
            return d

        def gla_products():
            yield from dense("w_in", 0, cols(O_GK + 128), h, out_scaled(g_k[:, 1, :], 1.0))
            tok_gk[1] = last_out()
            for j in range(2):
                yield from dense("w_in", 0, cols(O_GQ + 128 * j), h, out_scaled(g_q[:, j, :], 0.125))
                tok_gq[j] = last_out()

            def v_out(b, tb, tok):
                a = act(g_v[:, tb, :], b[:, 0:256], ACT.Copy, tok, stat["t"], scale=rtok[:, tb:tb + 1])
                tok_gv.append(a)
                return a
            yield from dense_tok("w_in", range(NK), cols(O_GV, 256), h, v_out)

        def gate_products():
            for j in range(2):
                yield from dense("w_in", 0, cols(O_GG + 128 * j), h, out_scaled(g_g[:, j, :], 0.5))
                tok_gg[j] = silu_in_place(g_g[:, j, :], last_out(), tmp_ring)

        def pool_means():
            z = [PO(lambda e, b=b: e.memset(b[:, :, 0:16], 0.0)) for b in (p_u, *p_a)]
            src, w = p_u, 1
            t = [pu_tok, z]
            C = slice(16, 16 + T)
            for step in range(4):
                dst = p_a[step % 2]
                t = tt(PO, dst[:, :, C], src[:, :, C], src[:, :, 16 - w:16 - w + T], ALU.add, t, p_tok)
                w *= 2
                j, r = step // 2, slice(64 * (step % 2), 64 * (step % 2) + 64)
                tp = p_d[r, j, :]
                x1 = tt(PO, tp, dst[r, j, C], icnt[r, j, :], ALU.mult, t, consts)
                x2 = tt(PO, tp, tp, p_u[r, j, C], ALU.subtract, x1)
                src = dst
                p_tok.append(x2)

        def pool_out():
            for j in range(2):
                slot = t_ring.take()
                tok = mm(slot.buf[:, :], wp_sb[:, j, :], p_d[:, j, :], True, True, p_tok, slot.free, consts,
                         tell=True)
                t1 = tmp_ring.take()
                a = act(t1.buf[:, :], slot.buf[:, :], ACT.Copy, tok, t1.free, scale=vec("pool_scale", j))
                slot.release(a)
                e = split_act(MH[:, j, :], ML[:, j, :], t1.buf[:, :], None, a, f_aug)
                t1.release(e)
                mix[j] = (MH[:, j, :], ML[:, j, :], e)
                yield

        p_tok = []
        p_d = sub("p_d", [128, 2, T], F32, 68)

        p_ring = Ring(Pb)
        pt_ring = Ring(PTb)
        st_ring = Ring([small[:, 4 * i:4 * i + 4] for i in range(8)])

        def attention(pairs, p_ring, pt_ring, yt_ring):
            to_b, to_c, to_d = [], [], []

            def step_b():
                u = to_b.pop(0)
                slot, pt = t_ring.take(), pt_ring.take()
                for kb in range(u["i"] + 1):
                    tok = PE(lambda e, kb=kb, b=slot.buf, p=u["p"]: nc.tensor.transpose(
                        b[:, kb * 128:kb * 128 + 128], p.buf[:, kb * 128:kb * 128 + 128], ident[:, :]),
                        u["exp"], slot.free, consts, tell=kb == u["i"])
                u["p"].release(tok)
                n = 128 * (u["i"] + 1)
                a = act(pt.buf[:, 0:n], slot.buf[:, 0:n], ACT.Copy, tok, pt.free)
                slot.release(a)
                u["pt"], u["moved"] = pt, a
                to_c.append(u)

            def step_c():
                u = to_c.pop(0)
                slot, pt = y_ring.take(), u["pt"]
                for kb in range(u["i"] + 1):
                    v_ap, v_tok = u["v"](kb)
                    tok = mm(slot.buf[:, 0:64], pt.buf[:, kb * 128:kb * 128 + 128], v_ap, kb == 0,
                             kb == u["i"], u["moved"], v_tok, slot.free, tell=kb == u["i"])
                pt.release(tok)
                st = u["st"]
                r = st.buf[:, 2:3]
                d = DV(lambda e: e.reciprocal(r, st.buf[:, 1:2]), u["exp"])
                yt, hl, i = u["yt"], u["hl"], u["i"]
                d = ts(DV, yt.buf[:, i, 64 * hl:64 * hl + 64], slot.buf[:, 0:64], r, None, ALU.mult, None, tok, d,
                       yt.free)
                st.release(d)
                slot.release(d)
                if hl == 1 and i == 3:
                    to_d.append((yt, d, u["finish"]))

            def step_d():
                yt, d, finish = to_d.pop(0)
                slot = t_ring.take()
                for i in range(4):
                    tok = PE(lambda e, i=i, b=slot.buf: nc.tensor.transpose(
                        b[:, i * 128:i * 128 + 128], yt.buf[:, i, :], ident[:, :]), d, slot.free, tell=i == 3)
                yt.release(tok)
                slot.release(finish(slot.buf, tok))

            for ready, begin in pairs:
                while not ready():
                    yield
                heads, finish = begin()
                yt = yt_ring.take()
                for hl, (scores_of, v_of) in enumerate(heads):
                    for i in range(4):
                        if to_d:
                            step_d()
                        n = 128 * (i + 1)
                        slot, st, p = s_ring.take(), st_ring.take(), p_ring.take()
                        nb, l, mx = st.buf[:, 0:1], st.buf[:, 1:2], st.buf[:, 3:4]
                        got = scores_of(i, slot, p, mx, st.free)
                        if got[0] == "moved":
                            slot.release(got[1])
                            src = p.buf[:, 0:n]
                            d = ts(DV, nb, mx, -1.0, None, ALU.mult, None, got[1])
                        else:
                            src = slot.buf[:, 0:n]
                            d = DV(lambda e, nb=nb, src=src: e.tensor_reduce(nb, src, AX, ALU.max, negate=True),
                                   got[1], st.free)
                        a = act(p.buf[:, 0:n], src, ACT.Exp, d, p.free, bias=nb, scale=1.0, acc=l)
                        if got[0] != "moved":
                            slot.release(a)
                        to_b.append({"i": i, "hl": hl, "p": p, "exp": a, "st": st, "yt": yt, "v": v_of,
                                     "finish": finish})
                        yield
                        if len(to_b) > 1:
                            step_b()
                        if len(to_c) > 1:
                            step_c()
                        yield
            while to_b or to_c or to_d:
                if to_d:
                    step_d()
                if to_b:
                    step_b()
                    yield
                if to_c:
                    step_c()
                    yield

        def causal(slot, i, which, tok):
            return mm(slot.buf[:, i * 128:i * 128 + 128], identb[:, 0, :], identb[:, which, :], False, True,
                      tell=True)

        fq_ring = Ring(f_qk)
        fox_in = {}
        fv_tok = []

        def fox_products(p):
            (slot,) = yield from taken(fq_ring)
            qk_free = slot.free
            toks = []

            def done(dst, k):
                def f(b, tok):
                    d = stt(DV, dst, b[:, :], k, Rb[:, :], ALU.mult, ALU.mult, tok, stat["b"], qk_free,
                            p_tok)
                    toks.append(d)
                    return d
                return f
            yield from dense("w_in", 0, cols(O_FQ + 128 * p), h, done(slot.buf[:, 0, :], 0.125))
            yield from dense("w_in", 0, cols(O_FK + 128 * p), h, done(slot.buf[:, 1, :], 1.0))
            fox_in[p] = (slot, toks)

        def fox_v():
            for c2 in range(2):
                def v_out(b, tb, tok, c2=c2):
                    a = act(f_v[:, tb, c2 * 256:c2 * 256 + 256], b[:, 0:256], ACT.Copy, tok, stat["t"], p_tok,
                            scale=rtok[:, tb:tb + 1])
                    fv_tok.append(a)
                    return a
                yield from dense_tok("w_in", range(NK), cols(O_FV + 256 * c2, 256), h, v_out)

        def fox_pair(p):
            slot_in, tin = fox_in[p]

            def head(hl):
                hd = 2 * p + hl
                r = slice(64 * hl, 64 * hl + 64)
                fr_ = slice(32 * (hd % 4), 32 * (hd % 4) + 6)

                def scores(i, slot, pbuf, mx, free):
                    n = 128 * (i + 1)
                    qs = slice(i * 128, i * 128 + 128)
                    mm(slot.buf[:, 0:n], slot_in.buf[r, 0, qs], slot_in.buf[r, 1, 0:n], True, False, tin,
                       slot.free)
                    mm(slot.buf[:, 0:n], f_lq[fr_, hd // 4, qs], f_lk[fr_, hd // 4, 0:n], False, False, f_aug)
                    tok = causal(slot, i, 1, None)
                    if hl == 1 and i == 3:
                        slot_in.release(tok)
                    return ("psum", tok)

                def v_of(kb):
                    return f_v[:, kb, hd * 64:hd * 64 + 64], fv_tok
                return scores, v_of

            def finish(b, tok):
                t1 = tmp_ring.take()
                a = act(t1.buf[:, :], b[:, :], ACT.Copy, tok, t1.free)
                e = split_act(MH[:, 4 + p, :], ML[:, 4 + p, :], t1.buf[:, :], None, a, g_last["done"])
                t1.release(e)
                mix[4 + p] = (MH[:, 4 + p, :], ML[:, 4 + p, :], e)
                return a
            return [head(0), head(1)], finish

        def chain(*gens):
            for g in gens:
                yield from g

        gla_front(0)
        gla_front(1)
        pool_means()
        run(gla_products())
        run(fox_v())
        run(pool_out())
        pool_pe = [(PE.sem, PE.n)]
        run(fox_products(0))
        for s in range(2):
            p_ring.free[s] = [f_aug, tokF, pool_pe]
            pt_ring.free[s] = [f_aug, tokF, pool_pe]
        yt_ring = Ring([sub(f"f_y{i}", [128, 4, 128], F32, 84 + 2 * i) for i in range(2)], p_tok)

        sx = Sum(acc[0], [stat["b"], stat["c"]])
        h2 = [None] * 8
        hold = []

        def add_to_x(m, sum_, gname, hlist, more=None):
            def done(b, tok):
                d = tt(DV, X[:, m, :], X[:, m, :], b[:, :], ALU.add, tok)
                if sum_ is not None:
                    sum_.add(X[:, m, :], None, d)
                    if more is not None:
                        more(m, d)
                    e = split_act(HH[:, m, :], HL[:, m, :], X[:, m, :], gname(m), d, hold)
                    hlist[m] = (HH[:, m, :], HL[:, m, :], e)
                return d
            return done

        def fox_side():
            for p in range(1, 4):
                yield from fox_products(p)
            yield from gate_products()
            yield from gla_out()
            hold[:] = [(PE.sem, PE.n)]
            for m in range(8):
                yield from dense("w_o", 0, cols(128 * m), mix, add_to_x(m, sx, lambda m: vec("ln2", m), h2))

        def with_rounds(gen, rounds):
            for x in gen:
                next(rounds, None)
                yield x
            for _ in rounds:
                yield

        weave(with_rounds(attention([(lambda p=p: p in fox_in, lambda p=p: fox_pair(p)) for p in range(4)],
                                    p_ring, pt_ring, yt_ring), chain(gla_pair(0), gla_pair(1))),
              fox_side(), [1.5] * 20 + [0.4])
        hold_rb = [(DV.sem, DV.n), (AC.sem, AC.n)]

        g_ring, sg_ring, a_ring = Ring(fg), Ring(fs), Ring(fa)
        first = [True]
        ffn = {}

        def ffn_norm():
            slot, tok = total(sx)
            ffn["a"], ffn["b"] = rsqrt(Rb[:, :], slot.buf[:, :], D, tok, hold_rb)
            slot.release(ffn["a"])
        region = [(PE.sem, PE.n), (DV.sem, DV.n), (AC.sem, AC.n)]
        pending = {}
        gdown = None
        for half in range(2):
            gu = []
            for j in range(FH):
                col = (half * FH + j) * 128
                gs, ss, us = g_ring.take(), sg_ring.take(), a_ring.take()

                def gate_out(b, tok, gs=gs, ss=ss):
                    d = stt(DV, gs.buf[:, :], b[:, :], 0.5, Rb[:, :], ALU.mult, ALU.mult, tok, ffn["b"], gs.free,
                            region)
                    a = act(ss.buf[:, :], gs.buf[:, :], ACT.Tanh, d, ss.free)
                    pending["g"] = stt(DV, gs.buf[:, :], ss.buf[:, :], 1.0, gs.buf[:, :], ALU.add, ALU.mult, a)
                    ss.release(pending["g"])
                    return d

                def up_out(b, tok, gs=gs, us=us, j=j):
                    d = tt(DV, us.buf[:, :], b[:, :], Rb[:, :], ALU.mult, tok, us.free)
                    q = tt(PO, us.buf[:, :], us.buf[:, :], gs.buf[:, :], ALU.mult, d, pending["g"])
                    gs.release(q)
                    e = split_act(GH[:, j, :], GL[:, j, :], us.buf[:, :], None, q, gdown)
                    us.release(e)
                    gu.append((GH[:, j, :], GL[:, j, :], e))
                    return d
                gen = dense("w_gu", 0, cols(col), h2, gate_out)
                if first[0]:
                    first[0] = False
                    next(gen)
                    next(gen)
                    ffn_norm()
                run(gen)
                run(dense("w_gu", 0, cols(DFF + col), h2, up_out))
            if half == 0:
                for m in range(8):
                    run(dense("w_down", 0, cols(128 * m), gu, add_to_x(m, None, None, None)))
                gdown = [(PE.sem, PE.n)]
            else:
                sx = Sum(acc[0], [ffn["a"]])
                sw = Sum(acc[1], None)
                h3 = [None] * 8
                hold[:] = [(PE.sem, PE.n)]

                def gg(m):
                    return gprod[:, m:m + 1]
                gprod = rtok[:, 8:16]
                lf = VEC["ln_f"][0]
                ng = VEC["norm_g_2"][0]
                gp = tt(DV, gprod, V[:, lf:lf + 8], V[:, ng:ng + 8], ALU.mult, vtok)
                hold.append(gp)

                def more(m, d):
                    sw.add(X[:, m, :], vec("ln_f", m), d)
                for m in range(8):
                    run(dense("w_down", FH, cols(128 * m), gu, add_to_x(m, sx, gg, h3, more=more)))

        region = [(PE.sem, PE.n), (DV.sem, DV.n), (AC.sem, AC.n)]
        b2 = {}

        def norm2():
            s1, k1 = total(sx)
            s2, k2 = total(sw)
            t1 = tmp_ring.take()
            a = act(t1.buf[:, :], s1.buf[:, :], ACT.Ln, k1, t1.free, region, scale=1.0 / D, bias=eps[:, :])
            s1.release(a)
            b2["f"] = act(Rf[:, :], t1.buf[:, :], ACT.Exp, a, scale=-0.5)
            a2 = act(Rb[:, :], t1.buf[:, :], ACT.Exp, a, scale=-1.0)
            d = tt(DV, Rb[:, :], Rb[:, :], s2.buf[:, :], ALU.mult, a2, k2)
            s2.release(d)
            a = act(Rb[:, :], Rb[:, :], ACT.Ln, d, scale=1.0 / D, bias=eps[:, :])
            d = tt(DV, Rb[:, :], Rb[:, :], t1.buf[:, :], ALU.add, a)
            t1.release(d)
            b2["b"] = act(Rb[:, :], Rb[:, :], ACT.Exp, d, scale=-0.5)
            s1, k1 = total_tok([sx, sw])
            a = act(rtok[:, 4:8], s1.buf[:, 0:4], ACT.Ln, k1, scale=1.0 / D, bias=eps[:, :])
            a2 = act(rtok[:, 0:4], rtok[:, 4:8], ACT.Exp, a, scale=-1.0)
            d = tt(DV, rtok[:, 0:4], rtok[:, 0:4], s1.buf[:, 4:8], ALU.mult, a2)
            s1.release(d)
            a = act(rtok[:, 0:4], rtok[:, 0:4], ACT.Ln, d, scale=1.0 / D, bias=eps[:, :])
            d = tt(DV, rtok[:, 0:4], rtok[:, 0:4], rtok[:, 4:8], ALU.add, a)
            b2["t"] = act(rtok[:, 0:4], rtok[:, 0:4], ACT.Exp, d, scale=-0.5)

        def scaled(dst, k, rb=None, rows=slice(0, 128), after=None, box=None, key=None, both=None):
            def done(b, tok):
                d = stt(DV, dst, b[rows, :], k, (rb or Rb)[rows, :], ALU.mult, ALU.mult, tok, b2["b"], after,
                        region)
                if box is not None:
                    box[key] = d
                return d
            return done

        ix = {}
        gen = dense("w_in_2", 0, cols(P_KI, 32) + cols(P_WI, 8) + (-1,) * 24 + cols(P_KR, 32)
                    + cols(P_KR + 16, 16) + cols(P_KR, 16), h3,
                    scaled(i_s[:, :], 1.0, box=ix, key="s"))
        next(gen)
        next(gen)
        norm2()
        run(gen)
        lo_ = landing()
        SP.dma(lo_, lambda e: e.dma_start(flip[:, :], cf[:, 896:1024]), region)
        SP.dma(lo_, lambda e: e.dma_start(oh[:, :], coh), region)
        ohk = SP.dma(lo_, lambda e: e.dma_start(rbs[:, :], relb), region)
        for c in range(2):
            s = t_ring.take()
            tok = mm(s.buf[0:8, 0:320], rbs[:, :], oh[:, 320 * c:320 * c + 320], True, True, ohk, s.free,
                     tell=True)
            a = act(brow[:, 320 * c:320 * c + 320], s.buf[0:8, 0:320], ACT.Copy, tok, region)
            s.release(a)
        ls = landing()
        bsent = SP.dma(ls, lambda e: e.dma_start(scratch, brow[:, :]), a)

        lk = landing()
        for g in range(4):
            ktok = SP.dma(lk, lambda e, g=g: e.dma_start(i_k[32 * g:32 * g + 32, :], i_s[0:32, :]), ix["s"],
                          region)
        ix["k"] = ktok
        t1, t2 = tmp_ring.take(), tmp_ring.take()
        d1 = tt(DV, t1.buf[64:96, :], i_s[64:96, :], RT[64:96, :], ALU.mult, ix["s"], consts, t1.free)
        d2 = tt(DV, t2.buf[64:96, :], i_s[96:128, :], RT[96:128, :], ALU.mult, t2.free)
        akr = []
        for s_ in range(4):
            akr.append(tt(DV, a_k[s_][64:96, :], t1.buf[64:96, :], t2.buf[64:96, :], ALU.add, d1, d2, region))
        akr = [tt(DV, a_k[s_][96:128, :], t1.buf[64:96, :], t2.buf[64:96, :], ALU.add, d1, d2, region)
               for s_ in range(4)][-1]
        t1.release(akr)
        t2.release(akr)
        s = t_ring.take()
        for tb in range(4):
            tok = PE(lambda e, tb=tb, b=s.buf: nc.tensor.transpose(
                b[:, 8 * tb:8 * tb + 8], i_s[32:40, tb * 128:tb * 128 + 128], ident[32:40, 32:40]),
                ix["s"], s.free, tell=tb == 3)
        ix["w"] = act(wi[:, :, :].rearrange("p a b -> p (a b)"), s.buf[:, 0:32], ACT.Copy, tok,
                      scale=8.0 ** -0.5)
        s.release(ix["w"])
        for j in range(2):
            run(dense("w_in_2", 0, cols(P_QI + 128 * j), h3,
                      scaled(i_q[:, j, :], 32.0 ** -0.5, box=ix, key=f"q{j}")))

        off = {1: 0, 2: 256, 3: 640}

        tops = behind["gens"]
        behind["per"] = 0.75

        def index_scores():
            for i in (3, 2, 1):
                n = 128 * (i + 1)
                sc = score[:, off[i]:off[i] + n]
                prev = None
                for hd in range(8):
                    r = slice(32 * (hd % 4), 32 * (hd % 4) + 32)
                    slot = s_ring.take()
                    tok = mm(slot.buf[:, 0:n], i_q[r, hd // 4, i * 128:i * 128 + 128], i_k[r, 0:n], True, True,
                             ix["k"], ix[f"q{hd // 4}"], slot.free, tell=True)
                    t = sq_ring.take()
                    a = act(t.buf[:, 0:n], slot.buf[:, 0:n], ACT.Relu, tok, t.free)
                    slot.release(a)
                    w = wi[:, i, hd:hd + 1]
                    if prev is None:
                        prev = ts(DV, sc, t.buf[:, 0:n], w, None, ALU.mult, None, a, ix["w"], region)
                    else:
                        prev = stt(DV, sc, t.buf[:, 0:n], w, sc, ALU.mult, ALU.add, a, prev)
                    t.release(prev)
                    yield
                prev = DV(lambda e, i=i, n=n: e.memset(score[0:64, off[i] + n - 64:off[i] + n], -BIG), prev)
                tops.append(top(i, n, sc, prev))

        def top(i, n, sc, prev):
            for rnd in range(16):
                d = DV(lambda e: e.max(m8[:, :], sc), prev)
                prev = DV(lambda e: e.match_replace(sc, m8[:, :], sc, GONE), d)
                yield
            ix[f"m{i}"] = ts(DV, nmask[:, off[i]:off[i] + n], sc, -2.0e38, -BIG, ALU.is_gt, ALU.mult, prev)

        slq, slk = Sum(acc[0], [(PE.sem, PE.n)]), Sum(acc[1], [(PE.sem, PE.n)])
        lq, lk_ = [], []

        def lat_out(c, hi, lo, gname, sum_, lst):
            def done(b, tok):
                t = tmp_ring.take()
                d = tt(DV, t.buf[:, :], b[:, :], Rb[:, :], ALU.mult, tok, b2["b"], t.free)
                s = sum_.add(t.buf[:, :], None, d)
                e = split_act(hi[:, c, :], lo[:, c, :], t.buf[:, :], vec(gname, c), d, region, bsent)
                t.release(e, s)
                lst.append((hi[:, c, :], lo[:, c, :], e))
                return d
            return done

        la = {}

        def latents():
            for c in range(3):
                yield from dense("w_in_2", 0, cols(P_QL + 128 * c), h3, lat_out(c, LQH, LQL, "g_q_lat_2", slq, lq))
            for c in range(2):
                yield from dense("w_in_2", 0, cols(P_CKV + 128 * c), h3,
                                 lat_out(c, LKH, LKL, "g_kv_lat_2", slk, lk_))
            s, k = total(slq)
            a, b = rsqrt(RQ[:, :], s.buf[:, :], 384, k, region)
            s.release(a)
            la["q"] = tt(DV, RQ[64:128, :], RQ[64:128, :], RT[64:128, :], ALU.mult, b)
            s, k = total(slk)
            a, la["k"] = rsqrt(RK[:, :], s.buf[:, :], 256, k, region)
            s.release(a)
            s, k = total_tok([slk])
            a, la["t"] = rtok_kv = rsqrt(rtok[:, 4:8], s.buf[:, 0:4], 256, k, b2["t"])
            s.release(a)
            yield

        va_tok = []

        def mla_v():
            for c2 in range(2):
                def v_out(b, tb, tok, c2=c2):
                    a = act(a_v[:, tb, c2 * 256:c2 * 256 + 256], b[:, 0:256], ACT.Copy, tok, la["t"], region,
                            scale=rtok[:, 4 + tb:5 + tb])
                    va_tok.append(a)
                    return a
                column = sum((cols(hd * 128 + 64, 64) for hd in range(4 * c2, 4 * c2 + 4)), ())
                yield from dense_tok("w_ukv_2", range(2), column, lk_, v_out)

        aq_ring = Ring(a_q)
        mla_in = {}
        z_ring = Ring(zb)

        def z_products(col, box, p):
            (z,) = yield from taken(z_ring)
            bx = {}
            yield from dense("w_in_2", 0, cols(col + 128 * p), h3, scaled(z.buf[:, :], 0.5, after=z.free, box=bx,
                                                                          key="z"))
            box[p] = (z, silu_in_place(z.buf[:, :], bx["z"], tmp_ring))

        za_in, zb_in = {}, {}

        def mla_products(p):
            sl = yield from taken(aq_ring, 2)
            tk = []

            def q_out(slot):
                def f(b, tok):
                    d = stt(DV, slot.buf[:, :], b[:, :], 96.0 ** -0.5, RQ[:, :], ALU.mult, ALU.mult, tok, la["q"],
                            slot.free, region)
                    tk.append(d)
                    return d
                return f

            def k_out(b, tok):
                for hl in range(2):
                    r = slice(64 * hl, 64 * hl + 64)
                    d = tt(DV, a_k[sl[hl].i][0:64, :], b[r, :], RK[r, :], ALU.mult, tok, la["k"], sl[hl].free)
                    tk.append(d)
                return d
            for hl in range(2):
                hd = 2 * p + hl
                yield from dense("w_uq_2", 0, cols(96 * hd, 96) + cols(96 * hd + 80, 16) + cols(96 * hd + 64, 16),
                                 lq, q_out(sl[hl]))
            yield from dense("w_ukv_2", 0, cols(256 * p, 64) + cols(256 * p + 128, 64), lk_, k_out)
            mla_in[p] = (sl, tk)
            yield from z_products(P_ZA, za_in, p)

        ya, yb = [None] * 4, [None] * 4

        def gated(p, hi, lo, lst, box):
            def finish(b, tok):
                z, ztok = box[p]
                t1 = tmp_ring.take()
                d = tt(DV, t1.buf[:, :], b[:, :], z.buf[:, :], ALU.mult, tok, ztok, t1.free)
                z.release(d)
                e = split_act(hi[:, p, :], lo[:, p, :], t1.buf[:, :], None, d, region)
                t1.release(e)
                lst[p] = (hi[:, p, :], lo[:, p, :], e)
                return d
            return finish

        def mla_pair(p):
            sl, tin = mla_in[p]

            def head(hl):
                hd = 2 * p + hl
                q, k = sl[hl].buf, a_k[sl[hl].i]

                def scores(i, slot, pbuf, mx, free):
                    n = 128 * (i + 1)
                    mm(slot.buf[:, 0:n], q[:, i * 128:i * 128 + 128], k[:, 0:n], True, False, tin, akr, slot.free)
                    tok = causal(slot, i, 2, None)
                    if i == 3:
                        sl[hl].release(tok)
                    return ("psum", tok)

                def v_of(kb):
                    return a_v[:, kb, hd * 64:hd * 64 + 64], va_tok
                return scores, v_of
            return [head(0), head(1)], gated(p, YAH, YAL, ya, za_in)

        weave(index_scores(), chain(latents(), mla_v(), mla_products(0)), 1.0)
        pc_ring, ptc_ring = Ring(Pc, region), Ring(PTc, region)
        yt3_free = [(PE.sem, PE.n), (DV.sem, DV.n), (AC.sem, AC.n), ktok]
        yt3_ring = Ring([sub(f"b_y{i}", [128, 4, 128], F32, 2 * i) for i in range(2)], yt3_free)

        b_ring = Ring(b_qk)
        dsa_in = {}
        bv_tok = []
        hold3 = []

        def dsa_v():
            hold3[:] = [(PE.sem, PE.n)]
            for c2 in range(2):
                def v_out(b, tb, tok, c2=c2):
                    a = act(b_v[:, tb, c2 * 256:c2 * 256 + 256], b[:, 0:256], ACT.Copy, tok, b2["t"], hold3,
                            scale=rtok[:, tb:tb + 1])
                    bv_tok.append(a)
                    return a
                yield from dense_tok("w_in_2", range(NK), cols(P_VB + 256 * c2, 256), h3, v_out)

        bias_in = {}
        t_land = [landing(), landing()]
        t_bias = Ring(b_t)
        raw_ring = Ring([sub(f"raw{i}", [128, T], F32, 4 + 2 * i) for i in range(2)])

        def dsa_row(hd):
            if hd > 7:
                return
            raw = raw_ring.take()
            src = scratch[hd:hd + 1, 0:T]
            ap = bass.AP(tensor=src.tensor, offset=src.offset, ap=[[1, 128], [1, T]])
            bt = SP.dma(t_land[hd % 2], lambda e, raw=raw, ap=ap: e.dma_start(raw.buf[:, :], ap), raw.free,
                        bsent)
            bias_in[hd] = (raw, bt)

        def dsa_bias(hd):
            if hd > 7:
                return
            raw, bt = bias_in[hd]
            bs = t_bias.take()
            slot = dense_ring.take()
            tok = mm(slot.buf[:, :], flip[:, :], raw.buf[:, :], True, True, bt, ohk, slot.free, tell=True)
            raw.release(tok, bt)
            a = act(bs.buf[:, :], slot.buf[:, :], ACT.Copy, tok, bs.free, hold3)
            slot.release(a)
            bias_in[hd] = (bs, a)

        def dsa_products(p):
            (s,) = yield from taken(b_ring)
            bx = {}
            yield from dense("w_in_2", 0, cols(P_QB + 128 * p), h3,
                             scaled(s.buf[:, 0, :], 0.125, after=[s.free, hold3], box=bx, key="q"))
            yield from dense("w_in_2", 0, cols(P_KB + 128 * p), h3,
                             scaled(s.buf[:, 1, :], 1.0, after=[s.free, hold3], box=bx, key="k"))
            dsa_in[p] = (s, [bx["q"], bx["k"]])
            yield from z_products(P_ZB, zb_in, p)

        def dsa_pair(p):
            s, tin = dsa_in[p]
            def head(hl):
                hd = 2 * p + hl
                r = slice(64 * hl, 64 * hl + 64)

                def scores(i, slot, pbuf, mx, free):
                    bs, bt = bias_in[hd]
                    n = 128 * (i + 1)
                    mm(slot.buf[:, 0:n], s.buf[r, 0, i * 128:i * 128 + 128], s.buf[r, 1, 0:n], True, False, tin,
                       slot.free)
                    if i == 0:
                        tok = causal(slot, 0, 2, None)
                    else:
                        tok = mm(slot.buf[:, 0:n], identb[:, 0, :], nmask[:, off[i]:off[i] + n], False, True,
                                 ix[f"m{i}"], tell=True)
                    d = DV(lambda e: e.tensor_tensor_reduce(
                        out=pbuf.buf[:, 0:n], in0=slot.buf[:, 0:n], in1=bs.buf[:, 512 - n:512], scale=1.0,
                        scalar=GONE, op0=ALU.add, op1=ALU.max, accum_out=mx), tok, bt, pbuf.free, free)
                    if i == 3:
                        bs.release(d)
                        if hl == 1:
                            s.release(tok)
                    if i == 0:
                        dsa_row(hd + 1)
                    if i == 2:
                        dsa_bias(hd + 1)
                    return ("moved", d)

                def v_of(kb):
                    return b_v[:, kb, hd * 64:hd * 64 + 64], bv_tok
                return scores, v_of
            return [head(0), head(1)], gated(p, YBH, YBL, yb, zb_in)

        def mla_side():
            for p in range(1, 4):
                yield from mla_products(p)
            yield from dsa_v()
            raw_ring.free = [list(f) for f in [yt3_free] * 2]
            dsa_row(0)
            yield from dsa_products(0)
            dsa_bias(0)
        weave(attention([(lambda p=p: p in za_in, lambda p=p: mla_pair(p)) for p in range(4)], pc_ring, ptc_ring,
                        yt3_ring), mla_side(), 1.0)
        while tops:
            run(tops.pop(0))
        region.append((PE.sem, PE.n))

        def dsa_side():
            for p in range(1, 4):
                yield from dsa_products(p)
        weave(attention([(lambda p=p: p in zb_in, lambda p=p: dsa_pair(p)) for p in range(4)], pc_ring, ptc_ring, yt3_ring), dsa_side(), 0.5)

        late = [(PE.sem, PE.n), (DV.sem, DV.n), (AC.sem, AC.n)]
        gt = Ring([Pc[0], Pc[1], PTc[0], PTc[1]], late)
        mt = Ring([zb[0], zb[1], RQ, RK], late)
        merged = []
        for m in range(8):
            halves = []
            for mat, col, y in (("w_o_a_2", P_GA, ya), ("w_o_b_2", P_GB, yb)):
                g = gt.take()
                q = mt.take()
                bx = {}

                def g_out(b, tok, g=g, bx=bx):
                    d = stt(DV, g.buf[:, :], b[:, :], 0.5, Rb[:, :], ALU.mult, ALU.mult, tok, g.free)
                    bx["g"] = act(g.buf[:, :], g.buf[:, :], ACT.Tanh, d)
                    return d

                def y_out(b, tok, g=g, q=q, bx=bx):
                    d = stt(DV, q.buf[:, :], g.buf[:, :], 1.0, b[:, :], ALU.add, ALU.mult, tok, bx["g"], q.free)
                    g.release(d)
                    bx["y"] = d
                    return d
                run(dense("w_in_2", 0, cols(col + 128 * m), h3, g_out))
                run(dense(mat, 0, cols(128 * m), y, y_out))
                halves.append((q, bx["y"]))
            (qa, ta), (qb, tb_) = halves
            d = tt(PO, qa.buf[:, :], qa.buf[:, :], qb.buf[:, :], ALU.add, ta, tb_)
            qb.release(d)
            e = split_act(MGH[:, m, :], MGL[:, m, :], qa.buf[:, :], 0.5, d, late)
            qa.release(e)
            merged.append((MGH[:, m, :], MGL[:, m, :], e))
            b2[f"x{m}"] = stt(DV, X[:, m, :], X[:, m, :], vec("ln_f", m), Rf[:, :], ALU.mult, ALU.mult, b2["f"])

        sx = Sum(acc[0], late)
        late = [(PE.sem, PE.n), (DV.sem, DV.n), (AC.sem, AC.n)]
        scaled_x = []
        o_x = sub("o_x", [128, 3, T], F32, 32)
        for m in range(8):
            def done(b, tok, m=m):
                d = tt(DV, X[:, m, :], X[:, m, :], b[:, :], ALU.add, tok, b2[f"x{m}"])
                sx.add(X[:, m, :], None, d, line=DV)
                if m < 3:
                    scaled_x.append(act(o_x[:, m, :], X[:, m, :], ACT.Copy, d, late, scale=vec("final_g_2", m)))
                return d
            run(dense("w_out_2", 0, cols(128 * m), merged, done))
        s, k = total(sx)
        a, b = rsqrt(Rb[:, :], s.buf[:, :], D, k)
        s.release(a)
        lout = landing()
        for m in range(8):
            if m in (0, 3, 6):
                c = m // 3
                d = tt(PO, o_x[:, c, :], o_x[:, c, :], Rb[:, :], ALU.mult, b, scaled_x[c])
                fin = SP.dma(lout, lambda e, c=c: e.dma_start(outT[:, c, :], o_x[:, c, :]), d)
                continue
            m = {1: 3, 2: 4, 4: 5, 5: 6, 7: 7}[m]
            d = stt(DV, X[:, m, :], X[:, m, :], vec("final_g_2", m), Rb[:, :], ALU.mult, ALU.mult, b)
            fin = SP.dma(lout, lambda e, m=m: e.dma_start(outT[:, m, :], X[:, m, :]), d)
        SP.todo.append(([fin, bsent], lambda e: None, None))
        while tile_no[0] < NTILES:
            tile_no[0] += 1
            plan.append((None, 0, ()))
        assert tile_no[0] == NTILES, tile_no

        block = ctx.enter_context(nc.Block())

        @block.sync
        def _(eng):
            SP.emit(eng)

        @block.scalar
        def _(eng):
            AC.emit(eng)

        @block.vector
        def _(eng):
            DV.emit(eng)

        @block.gpsimd
        def _(eng):
            PO.emit(eng)

        @block.tensor
        def _(eng):
            PE.emit(eng)
    return plan


def rope_table():
    half = 16
    freqs = np.float32(10000.0) ** (-np.arange(half, dtype=np.float32) / np.float32(half))
    ang = np.arange(T, dtype=np.float32)[:, None] * freqs.astype(np.float32)[None, :]
    cos, sin = np.cos(ang).T.astype(np.float32), np.sin(ang).T.astype(np.float32)
    out = np.ones((128, T), np.float32)
    out[64:80], out[80:96], out[96:112], out[112:128] = cos, cos, -sin, sin
    return out


def bucket_of(rel):
    nb, exact = 16, 8
    ret = (rel > 0).astype(np.int32) * nb
    n = np.abs(rel)
    nf = np.maximum(n, 1).astype(np.float32)
    large = exact + (np.log(nf / np.float32(exact)) / np.float32(np.log(128 / exact))
                     * np.float32(nb - exact)).astype(np.int32)
    large = np.minimum(large, nb - 1)
    return ret + np.where(n < exact, n, large)


def constants():
    p = np.arange(128)
    cf = np.zeros((128, 1024), np.float32)
    cf[:, 0:128] = np.eye(128, dtype=np.float32)
    cf[:, 128:640] = rope_table()
    keep = (p % 64)[:, None] <= np.arange(64)[None, :]
    cf[:, 640:704] = np.where(keep, np.float32(3.0e38), np.float32(0))
    cf[:, 704:768] = np.where(keep, np.float32(-3.0e38), np.float32(0))
    cf[:, 768:896] = (p[:, None] // 64 == p[None, :] // 64)
    cf[:, 896:1024] = np.eye(128, dtype=np.float32)[::-1]
    cph = np.zeros((128, 1536), np.float32)
    t1 = np.arange(1, T + 1)
    for g, w in enumerate((2, 4, 8, 16)):
        r = slice(64 * (g % 2), 64 * (g % 2) + 64)
        cph[r, 512 * (g // 2):512 * (g // 2) + 512] = np.float32(1) / np.minimum(t1, w).astype(np.float32)
    cph[:, 1024:1536] = (np.arange(T) % 64 != 0)
    coh = np.zeros((32, REL), np.float32)
    for n in range(REL - 1):
        coh[bucket_of(np.array(n - 127 - 384))[()], n] = 1.0
    coh[0, REL - 1] = 1.0
    from concourse import mybir as _mybir
    cb = np.zeros((128, 3, 128), np.float32)
    cb[:, 0] = np.eye(128)
    cb[:, 1] = np.where(p[None, :] <= p[:, None], 0.0, -BIG)
    cb[:, 2] = np.where(p[None, :] // 64 <= p[:, None] // 64, 0.0, -BIG)
    return cf, cph, coh, cb.astype(_mybir.dt.np(_mybir.dt.bfloat16))


def kernel(**inputs):
    import concourse.bacc as _bacc
    from concourse.bass_utils import run_bass_kernel_spmd as _run

    a = {k: np.asarray(v) for k, v in inputs.items()}
    nc = _bacc.Bacc("TRN2", target_bir_lowering=False, num_devices=1)
    arrays, order = {}, []

    def give(name, shape, dt):
        ap = nc.dram_tensor(name, shape, dt, kind="ExternalInput").ap()
        order.append(name)
        return ap

    NU = NTILES // UT
    wall = give("wall", (NU, 128, UT * 128), F32)
    xT = give("xT", (128, NK, T), F32)
    vecs = give("vecs", (128, NVEC), F32)
    wa = give("wa", (16, 256), F32)
    wp = give("wp", (128, 2, 128), F32)
    relb = give("relb", (32, 8), F32)
    cf = give("cf", (128, 1024), F32)
    cph = give("cph", (128, 1536), F32)
    coh = give("coh", (32, REL), F32)
    cb = give("cb", (128, 3, 128), BF16)
    scratch = nc.dram_tensor("scratch", (8, REL), F32, kind="Internal").ap()
    outT = nc.dram_tensor("outT", (128, NK, T), F32, kind="ExternalOutput").ap()
    plan = build(nc, wall, xT, vecs, wa, wp, relb, cf, cph, coh, cb, scratch, outT)

    w = np.zeros((NTILES, 128, 128), np.float32)
    for t, (name, k, column) in enumerate(plan):
        if name is None:
            continue
        m = a[name][0]
        c = np.array(column)
        have = c >= 0
        w[t][:, have] = m[128 * k:128 * k + 128][:, c[have]]
    arrays["wall"] = np.ascontiguousarray(w.reshape(NU, UT, 128, 128).transpose(0, 2, 1, 3)).reshape(
        NU, 128, UT * 128)
    arrays["xT"] = np.ascontiguousarray(a["x"][0].T.reshape(NK, 128, T).transpose(1, 0, 2))
    v = np.zeros((128, NVEC), np.float32)
    for name, (at, n) in VEC.items():
        g = a[name].reshape(-1)
        if name == "b_f":
            v[32:40, at] = g
        else:
            v[:, at:at + n] = g.reshape(n, 128).T
    arrays["vecs"] = v
    arrays["wa"] = np.ascontiguousarray(a["w_a_up"][0])
    wpp = np.zeros((128, 2, 128), np.float32)
    for g in range(4):
        r = slice(64 * (g % 2), 64 * (g % 2) + 64)
        wpp[r, g // 2, r] = a["w_pool"][0, g]
    arrays["wp"] = wpp
    arrays["relb"] = np.ascontiguousarray(a["rel_bias_2"])
    arrays["cf"], arrays["cph"], arrays["coh"], arrays["cb"] = constants()
    r = _run(nc, [arrays], core_ids=[0])
    y = r.results[0]["outT"]
    return np.ascontiguousarray(y.transpose(1, 0, 2).reshape(D, T).T)[None]
```

```python
from contextlib import ExitStack

import numpy as np

import concourse.bass as bass
from concourse import mybir
from concourse.alu_op_type import AluOpType as ALU

F32 = mybir.dt.float32
F32R = mybir.dt.float32r
BF16 = mybir.dt.bfloat16
ACT = mybir.ActivationFunctionType
AX = mybir.AxisListType.X

D = 1024
T = 512
NK = D // 128
DFF = 2816
FH = DFF // 2 // 128
EPS = 1e-6
UT = 8
NTILES = 1312
BIG = 1.0e30
GONE = -3.0e38
REL = 640

O_POOL, O_GQ, O_GK, O_GV, O_GG, O_GA = 0, 256, 512, 768, 1024, 1280
O_FQ, O_FK, O_FV, O_FF = 1296, 1808, 2320, 2832
P_QL, P_CKV, P_KR, P_ZA = 0, 384, 640, 672
P_QB, P_KB, P_VB, P_ZB = 1184, 1696, 2208, 2720
P_QI, P_KI, P_WI, P_GA, P_GB = 3232, 3488, 3520, 3528, 4552

VEC = {}
_at = 0
for _name, _n in (("ln1", 8), ("ln2", 8), ("ln_f", 8), ("norm_g_2", 8), ("final_g_2", 8),
                  ("pool_scale", 2), ("b_a", 2), ("gla_gn", 2), ("g_q_lat_2", 3),
                  ("g_kv_lat_2", 2), ("b_f", 1)):
    VEC[_name] = (_at, _n)
    _at += _n
NVEC = _at


def flat(tokens):
    out = []
    for t in tokens:
        if t is None:
            continue
        if isinstance(t, list):
            out += flat(t)
        else:
            out.append(t)
    return out


class Line:

    def __init__(self, sem, alone=False):
        self.sem, self.n, self.todo, self.seen, self.alone = sem, 0, [], {}, alone

    def waits(self, after):
        need = []
        for sem, value in flat(after):
            if self.seen.get(id(sem), 0) < value:
                self.seen[id(sem)] = value
                need.append((sem, value))
        return need

    def __call__(self, make, *after, tell=True):
        if self.alone and self.n:
            after = (*after, (self.sem, self.n))
        self.todo.append((self.waits(after), make, (self.sem, 1) if tell else None))
        if tell:
            self.n += 1
            return (self.sem, self.n)
        return None

    def dma(self, landing, make, *after):
        self.todo.append((self.waits(after), make, (landing.sem, 16)))
        landing.n += 16
        return (landing.sem, landing.n)

    def emit(self, eng):
        for need, make, tell in self.todo:
            for sem, value in need:
                eng.wait_ge(sem, value)
            ins = make(eng)
            if tell:
                ins.then_inc(*tell)


class Landing:

    def __init__(self, sem):
        self.sem, self.n = sem, 0


class Slot:
    def __init__(self, ring, i, free):
        self.ring, self.i, self.buf, self.free = ring, i, ring.bufs[i], free

    def release(self, *tokens):
        self.ring.free[self.i] = flat(tokens)


class Ring:

    def __init__(self, bufs, free=()):
        self.bufs, self.free, self.n = bufs, [list(free) for _ in bufs], 0

    def take(self):
        i = self.n % len(self.bufs)
        self.n += 1
        free = self.free[i]
        assert free is not None, "a buffer is taken before it was released"
        self.free[i] = None
        return Slot(self, i, free)


def taken(ring, count=1):
    while any(ring.free[(ring.n + i) % len(ring.bufs)] is None for i in range(count)):
        yield "not yet"
    return [ring.take() for _ in range(count)]


def weave(main, side, per):
    due = 0.0
    live = True
    rates = per if isinstance(per, list) else [per]
    for n, _ in enumerate(main):
        due += rates[min(n, len(rates) - 1)]
        while live and due >= 1:
            due -= 1
            got = next(side, "end")
            live = got != "end"
            if got == "not yet":
                due = 0.0
    for _ in side:
        pass


def build(nc, wall, xT, vecs, wa, wp, relb, cf, cph, coh, cb, scratch, outT):
    plan = []
    ctx = ExitStack()
    with ctx:
        KB = 1024
        base = 16896
        place = {"at": base}

        def at(name, shape, dt, off):
            return nc.alloc_sbuf_tensor_at(name, shape, dt, offset=off)

        def fixed(name, shape, dt=F32):
            size = int(np.prod(shape[1:])) * (2 if dt == BF16 else 4)
            size = (size + 31) // 32 * 32
            t = at(name, shape, dt, place["at"])
            place["at"] += size
            return t

        def sem(name):
            return ctx.enter_context(nc.semaphore(name))

        X = fixed("X", [128, NK, T])
        HH = fixed("HH", [128, NK, T], F32R)
        HL = fixed("HL", [128, NK, T], F32R)
        NST, NW = 3, 4
        WS = fixed("WS", [128, NST, UT * 128])
        WH = fixed("WH", [128, NW, UT * 128], F32R)
        WL = fixed("WL", [128, NW, UT * 128], F32R)
        ident = fixed("ident", [128, 128])
        RT = fixed("RT", [128, T])
        identb = fixed("identb", [128, 3, 128], BF16)
        ones = fixed("ones", [128, 128])
        V = fixed("V", [128, NVEC])
        eps = fixed("eps", [128, 1])
        Rb = fixed("Rb", [128, T])
        Rf_at = place["at"]
        Rf = fixed("Rf", [128, T])
        rtok = fixed("rtok", [128, 16])
        acc0 = fixed("acc0", [128, T])
        acc1_at = place["at"]
        acc = [acc0, fixed("acc1", [128, T])]
        sqb = [fixed("sq0", [128, T]), fixed("sq1", [128, T])]
        tmpb = [fixed("tmp0", [128, T]), fixed("tmp1", [128, T])]
        small = fixed("small", [128, 32])
        wi = fixed("wi", [128, 4, 8])
        m8 = fixed("m8", [128, 8])
        rbs = fixed("rbs", [32, 8])
        wa_sb = nc.alloc_sbuf_tensor_at("wa_sb", [16, 256], F32, offset=Rf_at)
        wp_sb = nc.alloc_sbuf_tensor_at("wp_sb", [128, 2, 128], F32, offset=Rf_at + KB)
        gmask = nc.alloc_sbuf_tensor_at("gmask", [128, 128], F32, offset=acc1_at)
        gones = nc.alloc_sbuf_tensor_at("gones", [128, 128], F32, offset=acc1_at + 512)
        R = place["at"]
        assert R + 92 * KB <= 229368, R + 92 * KB - 229368

        def sub(name, shape, dt, off):
            return at(name, shape, dt, R + int(off * KB))

        MH = sub("MH", [128, 8, T], F32R, 0)
        ML = sub("ML", [128, 8, T], F32R, 16)
        g_bc0 = sub("g_bc", [128, T], F32, 8)
        g_e = sub("g_e", [128, T], F32, 10)
        g_qi = sub("g_qi", [128, T], F32, 12)
        g_ki = sub("g_ki", [128, T], F32, 14)
        g_qe = sub("g_qe", [128, T], F32, 88)
        g_kh = sub("g_kh", [128, T], F32, 90)
        g_kt = sub("g_kt", [128, 4, 128], F32, 28)
        g_b2 = sub("g_b2", [128, T], F32, 30)
        g_q = sub("g_q", [128, 2, T], F32, 32)
        g_k = sub("g_k", [128, 2, T], F32, 36)
        g_g = sub("g_g", [128, 2, T], F32, 40)
        g_v = sub("g_v", [128, 4, 256], F32, 44)
        f_qk = [sub(f"f_qk{i}", [128, 2, T], F32, 48 + 4 * i) for i in range(2)]
        f_v = sub("f_v", [128, 4, T], F32, 56)
        f_lq = sub("f_lq", [128, 2, T], BF16, 64)
        f_lk = sub("f_lk", [128, 2, T], BF16, 66)
        Pb = [sub(f"Pb{i}", [128, T], F32, 68 + 2 * i) for i in range(2)]
        PTb = [sub(f"PTb{i}", [128, T], F32, 72 + 2 * i) for i in range(2)]
        g_S = sub("g_S", [128, 8, 128], F32, 76)
        g_at = sub("g_at", [128, 2, 4, 128], F32, 80)
        icnt = sub("icnt", [128, 2, T], F32, 84)
        rset = sub("rset", [128, T], F32, 88)
        p_u = sub("p_u", [128, 2, 16 + T], F32, 48)
        p_a = [sub(f"p_a{i}", [128, 2, 16 + T], F32, 52.25 + 4.25 * i) for i in range(2)]
        smz = sub("smz", [128, T], F32, 90)
        GH = sub("GH", [128, FH, T], F32R, 0)
        GL = sub("GL", [128, FH, T], F32R, 22)
        fg = [sub(f"fg{i}", [128, T], F32, 44 + 2 * i) for i in range(3)]
        fs = [sub(f"fs{i}", [128, T], F32, 50 + 2 * i) for i in range(3)]
        fa = [sub(f"fa{i}", [128, T], F32, 56 + 2 * i) for i in range(3)]
        i_q = sub("i_q", [128, 2, T], F32, 0)
        i_s = sub("i_s", [128, T], F32, 4)
        i_k = sub("i_k", [128, T], F32, 6)
        score = sub("score", [128, 1152], F32, 8)
        nmask = sub("nmask", [128, 1152], BF16, 12.75)
        LQH = sub("LQH", [128, 3, T], F32R, 16)
        LQL = sub("LQL", [128, 3, T], F32R, 22)
        LKH = sub("LKH", [128, 2, T], F32R, 28)
        LKL = sub("LKL", [128, 2, T], F32R, 32)
        b_qk = [sub(f"b_qk{i}", [128, 2, T], F32, 16 + 4 * i) for i in range(2)]
        b_v = sub("b_v", [128, 4, T], F32, 24)
        b_t = [sub(f"b_t{i}", [128, T], F32, 32 + 2 * i) for i in range(2)]
        YAH = sub("YAH", [128, 4, T], F32R, 36)
        YAL = sub("YAL", [128, 4, T], F32R, 44)
        a_q = [sub(f"a_q{i}", [128, T], F32, 52 + 4 * i) for i in range(4)]
        a_k = [sub(f"a_k{i}", [128, T], F32, 54 + 4 * i) for i in range(4)]
        a_v = sub("a_v", [128, 4, T], F32, 68)
        YBH = sub("YBH", [128, 4, T], F32R, 52)
        YBL = sub("YBL", [128, 4, T], F32R, 60)
        zb = [sub(f"zb{i}", [128, T], F32, 76 + 2 * i) for i in range(2)]
        Pc = [sub(f"Pc{i}", [128, T], F32, 80 + 2 * i) for i in range(2)]
        PTc = [sub(f"PTc{i}", [128, T], F32, 84 + 2 * i) for i in range(2)]
        RQ = sub("RQ", [128, T], F32, 88)
        RK = sub("RK", [128, T], F32, 90)
        oh = sub("oh", [32, REL], F32, 36)
        brow = sub("brow", [8, REL], F32, 39)
        MGH = sub("MGH", [128, 8, T], F32R, 0)
        MGL = sub("MGL", [128, 8, T], F32R, 16)

        bank = [ctx.enter_context(nc.psum_tensor(f"bank{i}", [128, 512], F32)) for i in range(8)]

        s_pe, s_act, s_dve, s_pool, s_sp = (sem(n) for n in ("pe", "act", "dve", "pool", "sp"))
        PE, AC, DV, PO, SP = Line(s_pe), Line(s_act), Line(s_dve), Line(s_pool, alone=True), Line(s_sp)
        stage_in = [Landing(sem(f"w_in{i}")) for i in range(NST)]
        nland = [0]

        def landing():
            nland[0] += 1
            return Landing(sem(f"land{nland[0]}"))

        dense_ring = Ring(bank[0:2])
        s_ring = Ring(bank[2:4])
        t_ring = Ring(bank[4:6])
        y_ring = Ring(bank[6:8])
        sq_ring = Ring(sqb)
        tmp_ring = Ring(tmpb)

        def mm(out, l, r, start, stop, *after, tell=False):
            return PE(lambda e: nc.tensor.matmul(out, l, r, start=start, stop=stop), *after, tell=tell)

        def act(out, in_, f, *after, bias=None, scale=None, acc=None):
            kw = {}
            if bias is not None:
                kw["bias"] = bias
            if scale is not None:
                kw["scale"] = scale
            if acc is not None:
                kw["accum_out"] = acc
            return AC(lambda e: nc.scalar.activation(out, in_, f, **kw), *after)

        def tt(line, out, a, b, op, *after):
            return line(lambda e: e.tensor_tensor(out, a, b, op), *after)

        def ts(line, out, a, s1, s2, op0, op1, *after):
            if op1 is None:
                return line(lambda e: e.tensor_scalar(out, a, s1, None, op0), *after)
            return line(lambda e: e.tensor_scalar(out, a, s1, s2, op0, op1), *after)

        def stt(line, out, a, s, b, op0, op1, *after):
            return line(lambda e: e.scalar_tensor_tensor(out, a, s, b, op0, op1), *after)

        def vec(name, c):
            return V[:, VEC[name][0] + c:VEC[name][0] + c + 1]

        def f32(ap):
            return ap.bitcast(F32)

        NU = NTILES // UT
        wst = {"ready": {}, "free": [None] * NW, "conv": 0, "dma": 0, "stage_free": [None] * NST,
               "landed": {}, "low": DV}

        def load_unit():
            u = wst["dma"]
            if u >= NU:
                return
            wst["dma"] += 1
            k = u % NST
            wst["landed"][u] = SP.dma(stage_in[k], lambda e: e.dma_start(WS[:, k, :], wall[u]),
                                      wst["stage_free"][k])

        def split_unit():
            u = wst["conv"]
            if u >= NU:
                return
            wst["conv"] += 1
            k, j = u % NST, u % NW
            a = act(WH[:, j, :], WS[:, k, :], ACT.Copy, wst["landed"][u], wst["free"][j])
            d = tt(wst["low"], WL[:, j, :], WS[:, k, :], f32(WH[:, j, :]), ALU.subtract, a)
            wst["free"][j] = "busy"
            wst["ready"][u] = d
            wst["stage_free"][k] = [d, wst["landed"][u]]
            load_unit()

        tile_no = [0]
        behind = {"gens": [], "due": 0.0, "per": 0.0}

        def go_behind():
            behind["due"] = behind["due"] + behind["per"] if behind["gens"] else 0.0
            while behind["due"] >= 1 and behind["gens"]:
                behind["due"] -= 1
                if next(behind["gens"][0], "end") == "end":
                    behind["gens"].pop(0)

        def next_tile(what):
            t = tile_no[0]
            tile_no[0] += 1
            plan.append(what)
            u = t // UT
            while wst["conv"] <= min(u + 2, NU - 1):
                split_unit()
            c = (t % UT) * 128
            j = u % NW
            return WH[:, j, c:c + 128], WL[:, j, c:c + 128], wst["ready"][u], t

        def tile_done(t, tok):
            if t % UT == UT - 1:
                wst["free"][(t // UT) % NW] = tok

        def cols(c0, n=128):
            return tuple(range(c0, c0 + n))

        def dense(mat, k0, column, rhs, done, steps=2, ring=None, later=None):
            slot = (ring or dense_ring).take()
            n = len(rhs)
            for k in range(n):
                part = rhs[k]
                while part is None or callable(part) and part() is None:
                    yield "not yet"
                    part = rhs[k]
                rh, rl, tok = part() if callable(part) else part
                wh, wl, ready, t = next_tile((mat, k0 + k, column))
                first, last = k == 0, k == n - 1
                end = last or t % UT == UT - 1
                mm(slot.buf[:, :], wh, rh, first, False, slot.free if first else None, ready, tok)
                mm(slot.buf[:, :], wh, rl, False, False)
                tok2 = mm(slot.buf[:, :], wl, rh, False, last, tell=end)
                if end:
                    wst["last_pe"] = tok2
                    tile_done(t, tok2)
                if k % steps == steps - 1 and not last:
                    go_behind()
                    yield
            if later is None:
                slot.release(done(slot.buf, tok2))
            else:
                later.append(lambda: slot.release(done(slot.buf, tok2)))
            yield

        def dense_tok(mat, ks, column, lhs, done):
            while tile_no[0] % 2:
                _, _, _, t = next_tile((None, 0, ()))
                tile_done(t, wst["last_pe"])
            tiles, starts = [], []
            for k in ks:
                a = next_tile((mat, k, column[:128]))
                b = next_tile((mat, k, column[128:]))
                starts.append(a[3])
                j, c = (a[3] // UT) % NW, (a[3] % UT) * 128
                tiles.append((WH[:, j, c:c + 256], WL[:, j, c:c + 256], a[2]))
            for tb in range(4):
                slot = dense_ring.take()
                cs = slice(tb * 128, tb * 128 + 128)
                for k, (wh, wl, ready) in enumerate(tiles):
                    hh, hl, tok = lhs[k]
                    first, last = k == 0, k == len(tiles) - 1
                    mm(slot.buf[:, 0:256], hh[:, cs], wh, first, False, slot.free if first else None,
                       ready, tok)
                    mm(slot.buf[:, 0:256], hh[:, cs], wl, False, False)
                    tok2 = mm(slot.buf[:, 0:256], hl[:, cs], wh, False, last, tell=last)
                    if k % 4 == 3 and not last:
                        go_behind()
                        yield
                slot.release(done(slot.buf, tb, tok2))
                if tb == 3:
                    wst["last_pe"] = tok2
                    for a in starts:
                        tile_done(a, tok2)
                        tile_done(a + 1, tok2)
                yield

        def split_act(hi, lo, src, g, *after, extra=None):
            if g is None:
                a = act(hi, src, ACT.Copy, *after)
                d = tt(DV, lo, src, f32(hi), ALU.subtract, a, *after)
            else:
                a = act(hi, src, ACT.Copy, *after, scale=g)
                d = stt(DV, lo, src, g, f32(hi), ALU.mult, ALU.subtract, a, *after)
            return d

        class Sum:
            def __init__(self, buf, free):
                self.buf, self.tok, self.free = buf, None, free

            def add(self, src, scale, *after, line=None):
                line = line or PO
                s = sq_ring.take()
                a = act(s.buf[:, :], src, ACT.Square, *after, s.free, scale=scale)
                if self.tok is None:
                    self.tok = line(lambda e: e.tensor_copy(self.buf[:, :], s.buf[:, :]), a, self.free)
                else:
                    self.tok = tt(line, self.buf[:, :], self.buf[:, :], s.buf[:, :], ALU.add, a, self.tok)
                s.release(self.tok)
                return a

        def total(sum_):
            slot = t_ring.take()
            tok = mm(slot.buf[:, :], ones[:, :], sum_.buf[:, :], True, True, sum_.tok, slot.free,
                     c_ones, tell=True)
            return slot, tok

        def total_tok(sums):
            slot = t_ring.take()
            for i, s in enumerate(sums):
                for tb in range(4):
                    last = i == len(sums) - 1 and tb == 3
                    tok = mm(slot.buf[:, 4 * i + tb:4 * i + tb + 1], s.buf[:, tb * 128:tb * 128 + 128],
                             ones[:, 0:1], True, True, s.tok, slot.free, c_ones, tell=last)
            return slot, tok

        def rsqrt(dst, src, n, *after):
            a = act(dst, src, ACT.Ln, *after, scale=1.0 / n, bias=eps[:, :])
            return a, act(dst, dst, ACT.Exp, a, scale=-0.5)

        c_ones = PO(lambda e: e.memset(ones[:, :], 1.0))
        c_eps = PO(lambda e: e.memset(eps[:, :], EPS))
        vtok = SP.dma(landing(), lambda e: e.dma_start(V[:, :], vecs))
        x_in = []
        for c in range(NK):
            x_in.append(SP.dma(landing(), lambda e, c=c: e.dma_start(X[:, c, :], xT[:, c, :])))
            if c in (0, 2, 4):
                load_unit()
        lc = landing()
        SP.dma(lc, lambda e: e.dma_start(ident[:, :], cf[:, 0:128]))
        SP.dma(lc, lambda e: e.dma_start(RT[:, :], cf[:, 128:640]))
        SP.dma(lc, lambda e: e.dma_start(identb[:, :, :], cb))
        SP.dma(lc, lambda e: e.dma_start(gmask[:, :], cf[:, 640:768]))
        SP.dma(lc, lambda e: e.dma_start(gones[:, :], cf[:, 768:896]))
        SP.dma(lc, lambda e: e.dma_start(wa_sb[:, :], wa))
        SP.dma(lc, lambda e: e.dma_start(wp_sb[:, :, :], wp))
        SP.dma(lc, lambda e: e.dma_start(icnt[:, :, :], cph[:, 0:1024].rearrange("p (a n) -> p a n", a=2)))
        consts = SP.dma(lc, lambda e: e.dma_start(rset[:, :], cph[:, 1024:1536]))

        act(small[:, 0:1], eps[:, :], ACT.Copy, c_eps)
        sx = Sum(acc[0], None)
        h = []
        for c in range(NK):
            d = split_act(HH[:, c, :], HL[:, c, :], X[:, c, :], vec("ln1", c), x_in[c], vtok)
            h.append((HH[:, c, :], HL[:, c, :], d))
            if c in (0, 2, 4):
                split_unit()
            sx.add(X[:, c, :], None, x_in[c], line=DV)

        stat = {}

        def norm1():
            s1, k1 = total(sx)
            s2, k2 = total_tok([sx])
            a1 = act(Rb[:, :], s1.buf[:, :], ACT.Ln, k1, c_eps, scale=1.0 / D, bias=eps[:, :])
            stat["c"] = act(rtok[:, 0:4], s2.buf[:, 0:4], ACT.Ln, k2, scale=1.0 / D, bias=eps[:, :])
            s1.release(a1)
            s2.release(stat["c"])
            stat["b"] = act(Rb[:, :], Rb[:, :], ACT.Exp, a1, scale=-0.5)
            stat["t"] = act(rtok[:, 0:4], rtok[:, 0:4], ACT.Exp, stat["c"], scale=-0.5)

        def run(gen):
            for _ in gen:
                pass

        def out_scaled(dst, k):
            def done(b, tok):
                d = stt(DV, dst, b[:, :], float(k), Rb[:, :], ALU.mult, ALU.mult, tok, stat["b"])
                out_tok.append(d)
                return d
            return done

        out_tok = []

        def last_out():
            return out_tok[-1]

        early = Ring([bank[0], bank[1], bank[6], bank[7]])
        firsts = [(cols(O_GA, 16) + (-1,) * 16 + cols(O_FF, 8) + (-1,) * 88, smz[:, :]),
                  (cols(O_POOL), p_u[:, 0, 16:16 + T]), (cols(O_POOL + 128), p_u[:, 1, 16:16 + T]),
                  (cols(O_GK), g_k[:, 0, :])]
        slots = [early.take() for _ in firsts]
        for k in range(NK):
            rh, rl, tok = h[k]
            for slot, (column, _) in zip(slots, firsts):
                wh, wl, ready, t = next_tile(("w_in", k, column))
                mm(slot.buf[:, :], wh, rh, k == 0, False, ready, tok)
                mm(slot.buf[:, :], wh, rl, False, False)
                slot.tok = mm(slot.buf[:, :], wl, rh, False, k == NK - 1, tell=True)
                wst["last_pe"] = slot.tok
                tile_done(t, slot.tok)
            if k == NK - 2:
                norm1()
        for slot, (_, dst) in zip(slots, firsts):
            slot.release(out_scaled(dst, 1.0)(slot.buf, slot.tok))
        dense_ring.free = early.free[0:2]
        y_ring.free = early.free[2:4]
        sm_tok, pu_tok, tok_gk0 = out_tok[0], out_tok[1:3], out_tok[3]

        fr = slice(32, 40)
        zf = smz[fr, :]
        q1, q2 = tmp_ring.take(), sq_ring.take()
        w1, w2 = q1.buf[fr, :], q2.buf[fr, :]
        bf = V[fr, VEC["b_f"][0]:VEC["b_f"][0] + 1]
        d1 = act(w1, zf, ACT.Abs, sm_tok, q1.free, vtok, bias=bf)
        a1 = act(w1, w1, ACT.Exp, d1, scale=-1.0)
        a1 = act(w1, w1, ACT.Ln, a1, bias=1.0)
        d2 = ts(DV, w2, zf, bf, 0.0, ALU.add, ALU.min, sm_tok, q2.free)
        d2 = tt(DV, w2, w2, w1, ALU.subtract, d2, a1)
        F = sub("F", [128, T], F32, 72)
        parts = [sub(f"part{j}", [128, T], BF16, 16 + j) for j in range(3)]
        negs = [sub(f"neg{j}", [128, T], BF16, 19 + j) for j in range(3)]
        one = PO(lambda e: e.memset(w1, 1.0), d2)
        dF = DV(lambda e: e.tensor_tensor_scan(F[fr, :], w1, w2, 0.0, ALU.mult, ALU.add), one, d2)
        q1.release(dF)
        m1 = PO(lambda e: e.memset(f_lq[:, :, :], 1.0))
        m2 = PO(lambda e: e.memset(f_lk[:, :, :], 1.0))
        lF = landing()
        tokF = dF
        for j in range(3):
            part, neg = parts[j], negs[j]
            dp = DV(lambda e, part=part: e.tensor_copy(part[fr, :], F[fr, :]), tokF)
            dn = ts(DV, neg[fr, :], part[fr, :], -1.0, None, ALU.mult, None, dp)
            if j < 2:
                tokF = tt(DV, F[fr, :], F[fr, :], part[fr, :], ALU.subtract, dp)
            for src, dst, row, mk in ((part, f_lq, 3 + j, m1), (neg, f_lk, j, m2)):
                for hh in range(2):
                    f_aug = SP.dma(lF, lambda e, src=src, dst=dst, row=row, hh=hh: e.dma_start(
                        dst[row:row + 97:32, hh, :], src[32 + 4 * hh:36 + 4 * hh, :]), dp, dn, mk)
        q2.release(tokF, dF)

        def gla_front(hp):
            gb = (g_bc0, g_b2)[hp]
            t1, t2 = tmp_ring.take(), sq_ring.take()
            slot = t_ring.take()
            tok = mm(slot.buf[:, :], wa_sb[0:16, hp * 128:hp * 128 + 128], smz[0:16, :], True, True,
                     sm_tok, consts, slot.free, tell=True)
            d1 = act(t1.buf[:, :], slot.buf[:, :], ACT.Abs, tok, t1.free, vtok, bias=vec("b_a", hp))
            d2 = ts(DV, t2.buf[:, :], slot.buf[:, :], vec("b_a", hp), 0.0, ALU.add, ALU.min, d1, t2.free)
            slot.release(d2)
            a = act(t1.buf[:, :], t1.buf[:, :], ACT.Exp, d1, scale=-1.0)
            a = act(t1.buf[:, :], t1.buf[:, :], ACT.Ln, a, bias=1.0)
            d = tt(DV, t2.buf[:, :], t2.buf[:, :], t1.buf[:, :], ALU.subtract, d2, a)
            t1.release(d)
            g_last["bc", hp] = DV(lambda e: e.tensor_tensor_scan(gb[:, :], rset[:, :], t2.buf[:, :], 0.0,
                                                                 ALU.mult, ALU.add), d, consts)
            t2.release(g_last["bc", hp])

        def gla_pair(hp):
            g_bc, w, dbc = (g_bc0, g_b2)[hp], g_last.get("done"), [g_last["bc", 0], g_last["bc", 1]]
            bc = g_bc[:, :].rearrange("p (n c) -> p n c", c=64)
            ref = bc[:, :, 31:32].broadcast_to([128, 8, 64])
            lst = bc[:, :, 63:64].broadcast_to([128, 8, 64])
            t3 = tmp_ring.take()
            v3 = t3.buf[:, :].rearrange("p (n c) -> p n c", c=64)
            d = tt(DV, v3, bc, ref, ALU.subtract, dbc, t3.free)
            a = act(g_e[:, :], t3.buf[:, :], ACT.Exp, d, w, scale=1.0 / 16)
            q = g_q[:, hp, :]
            k = g_k[:, hp, :]
            yield
            dq = tt(DV, g_qi[:, :], q, g_e[:, :], ALU.mult, a, tok_gq[hp], w)
            a = act(g_e[:, :], t3.buf[:, :], ACT.Exp, dq, scale=-1.0 / 16)
            yield
            dk = tt(DV, g_ki[:, :], k, g_e[:, :], ALU.mult, a, tok_gk[hp])
            t3.release(a)
            a = act(g_e[:, :], g_bc[:, :], ACT.Exp, dk, dbc, scale=1.0 / 16)
            yield
            dqe = tt(DV, g_qe[:, :], q, g_e[:, :], ALU.mult, a)
            t4 = tmp_ring.take()
            v4 = t4.buf[:, :].rearrange("p (n c) -> p n c", c=64)
            d = tt(DV, v4, lst, bc, ALU.subtract, dbc, t4.free)
            a4 = act(t4.buf[:, :], t4.buf[:, :], ACT.Exp, d, scale=1.0 / 16)
            yield
            dkh = tt(DV, g_kh[:, :], k, t4.buf[:, :], ALU.mult, a4)
            t4.release(dkh)
            yield
            yield
            slot = t_ring.take()
            for tb in range(4):
                tok = PE(lambda e, tb=tb, b=slot.buf: nc.tensor.transpose(
                    b[:, tb * 128:tb * 128 + 128], g_kh[:, tb * 128:tb * 128 + 128], ident[:, :]),
                    dkh, slot.free, consts, tell=tb == 3)
            akt = act(g_kt[:, :, :].rearrange("p a n -> p (a n)"), slot.buf[:, :], ACT.Copy, tok)
            slot.release(akt)
            yield
            datt = []
            for hl in range(2):
                slot = s_ring.take()
                for n in range(8):
                    r = slice(64 * hl, 64 * hl + 64)
                    o = slice(64 * (n % 2), 64 * (n % 2) + 64)
                    tok = mm(slot.buf[o, 64 * (n // 2):64 * (n // 2) + 64], g_ki[r, 64 * n:64 * n + 64],
                             g_qi[r, 64 * n:64 * n + 64], True, True, dk, dq, slot.free, tell=n == 7)
                slot.tok = tok
                for par in range(2):
                    o = slice(64 * par, 64 * par + 64)
                    src = slot.buf[o, 0:256].rearrange("p (n c) -> p n c", c=64)
                    dst = g_at[o, hl, :, 64 * par:64 * par + 64]
                    hi = gmask[o, 0:64].unsqueeze(1).broadcast_to([64, 4, 64])
                    lo = gmask[o, 64:128].unsqueeze(1).broadcast_to([64, 4, 64])
                    x1 = tt(DV, dst, src, hi, ALU.min, slot.tok, consts, g_zero)
                    datt.append(tt(DV, dst, dst, lo, ALU.max, x1))
                slot.release(x1)
                yield
            kv = []
            for par in range(2):
                slot = s_ring.take()
                kv.append(slot)
                r = slice(64 * par, 64 * par + 64)
                for n4 in range(4):
                    tok = mm(slot.buf[:, n4 * 128:n4 * 128 + 128], g_kt[r, n4, :],
                             g_v[r, n4, hp * 128:hp * 128 + 128], True, True, akt, tok_gv, slot.free,
                             tell=n4 == 3)
                slot.tok = tok
            dS = g_zero
            first = [w, dbc]
            for n in range(7):
                slot = kv[n % 2]
                nd = []
                for hl in range(2):
                    r = slice(64 * hl, 64 * hl + 64)
                    src = slot.buf[r, (n // 2) * 128 + 64 * hl:(n // 2) * 128 + 64 * hl + 64]
                    nd.append(stt(DV, g_S[r, n + 1, 64 * hl:64 * hl + 64], g_S[r, n, 64 * hl:64 * hl + 64],
                                  g_e[r, 64 * n + 63:64 * n + 64], src, ALU.mult, ALU.add, slot.tok, dS,
                                  dqe, first))
                dS = nd[-1]
            kv[0].release(dS)
            kv[1].release(dS)
            yield
            yield
            slot = y_ring.take()
            for n4 in range(4):
                cs = slice(n4 * 128, n4 * 128 + 128)
                for hl in range(2):
                    mm(slot.buf[64 * hl:64 * hl + 64, cs], g_v[:, n4, (2 * hp + hl) * 64:(2 * hp + hl) * 64 + 64],
                       g_at[:, hl, n4, :], True, False, datt, slot.free, tok_gv)
                for par in range(2):
                    n = 2 * n4 + par
                    tok = mm(slot.buf[:, 64 * n:64 * n + 64], g_S[:, n, :], g_qe[:, 64 * n:64 * n + 64],
                             False, par == 1, dS, dqe, tell=True)
            sq = sq_ring.take()
            a = act(sq.buf[:, :], slot.buf[:, :], ACT.Square, tok, sq.free)
            o = g_q[:, hp, :]
            do = ts(DV, o, slot.buf[:, :], vec("gla_gn", hp), None, ALU.mult, None, a, tok)
            slot.release(do)
            ts_ = t_ring.take()
            tok = mm(ts_.buf[:, :], gones[:, :], sq.buf[:, :], True, True, a, ts_.free, g_ones, tell=True)
            t5 = tmp_ring.take()
            a, b = rsqrt(t5.buf[:, :], ts_.buf[:, :], 64, tok, t5.free)
            ts_.release(a)
            sq.release(tok)
            d = tt(DV, o, o, t5.buf[:, :], ALU.mult, b, do)
            t5.release(d)
            g_last["done"] = [d]
            g_last[hp] = d
            yield

        def gla_out():
            for hp in range(2):
                o = g_q[:, hp, :]
                d = tt(DV, o, o, g_g[:, hp, :], ALU.mult, g_last[hp], tok_gg[hp])
                e = split_act(MH[:, 2 + hp, :], ML[:, 2 + hp, :], o, None, d, f_aug)
                mix[2 + hp] = (MH[:, 2 + hp, :], ML[:, 2 + hp, :], e)
            yield

        g_ones = consts
        z1 = PO(lambda e: e.memset(g_S[:, :, :], 0.0))
        z2 = PO(lambda e: e.memset(g_at[:, :, :, :], 0.0))
        g_zero = [z1, z2]
        g_last = {}
        mix = [None] * 8
        tok_gq, tok_gk, tok_gg, tok_gv = [None] * 2, [tok_gk0, None], [None] * 2, []

        def silu_in_place(z, tok, ring):
            t = ring.take()
            a = act(t.buf[:, :], z, ACT.Tanh, tok, t.free)
            d = stt(DV, z, t.buf[:, :], 1.0, z, ALU.add, ALU.mult, a)
            t.release(d)
            return d

        def gla_products():
            yield from dense("w_in", 0, cols(O_GK + 128), h, out_scaled(g_k[:, 1, :], 1.0))
            tok_gk[1] = last_out()
            for j in range(2):
                yield from dense("w_in", 0, cols(O_GQ + 128 * j), h, out_scaled(g_q[:, j, :], 0.125))
                tok_gq[j] = last_out()

            def v_out(b, tb, tok):
                a = act(g_v[:, tb, :], b[:, 0:256], ACT.Copy, tok, stat["t"], scale=rtok[:, tb:tb + 1])
                tok_gv.append(a)
                return a
            yield from dense_tok("w_in", range(NK), cols(O_GV, 256), h, v_out)

        def gate_products():
            for j in range(2):
                yield from dense("w_in", 0, cols(O_GG + 128 * j), h, out_scaled(g_g[:, j, :], 0.5))
                tok_gg[j] = silu_in_place(g_g[:, j, :], last_out(), tmp_ring)

        def pool_means():
            z = [PO(lambda e, b=b: e.memset(b[:, :, 0:16], 0.0)) for b in (p_u, *p_a)]
            src, w = p_u, 1
            t = [pu_tok, z]
            C = slice(16, 16 + T)
            for step in range(4):
                dst = p_a[step % 2]
                t = tt(PO, dst[:, :, C], src[:, :, C], src[:, :, 16 - w:16 - w + T], ALU.add, t, p_tok)
                w *= 2
                j, r = step // 2, slice(64 * (step % 2), 64 * (step % 2) + 64)
                tp = p_d[r, j, :]
                x1 = tt(PO, tp, dst[r, j, C], icnt[r, j, :], ALU.mult, t, consts)
                x2 = tt(PO, tp, tp, p_u[r, j, C], ALU.subtract, x1)
                src = dst
                p_tok.append(x2)

        def pool_out():
            for j in range(2):
                slot = t_ring.take()
                tok = mm(slot.buf[:, :], wp_sb[:, j, :], p_d[:, j, :], True, True, p_tok, slot.free, consts,
                         tell=True)
                t1 = tmp_ring.take()
                a = act(t1.buf[:, :], slot.buf[:, :], ACT.Copy, tok, t1.free, scale=vec("pool_scale", j))
                slot.release(a)
                e = split_act(MH[:, j, :], ML[:, j, :], t1.buf[:, :], None, a, f_aug)
                t1.release(e)
                mix[j] = (MH[:, j, :], ML[:, j, :], e)
                yield

        p_tok = []
        p_d = sub("p_d", [128, 2, T], F32, 68)

        p_ring = Ring(Pb)
        pt_ring = Ring(PTb)
        st_ring = Ring([small[:, 4 * i:4 * i + 4] for i in range(8)])

        def attention(pairs, p_ring, pt_ring, yt_ring):
            to_b, to_c, to_d = [], [], []

            def step_b():
                u = to_b.pop(0)
                slot, pt = t_ring.take(), pt_ring.take()
                for kb in range(u["i"] + 1):
                    tok = PE(lambda e, kb=kb, b=slot.buf, p=u["p"]: nc.tensor.transpose(
                        b[:, kb * 128:kb * 128 + 128], p.buf[:, kb * 128:kb * 128 + 128], ident[:, :]),
                        u["exp"], slot.free, consts, tell=kb == u["i"])
                u["p"].release(tok)
                n = 128 * (u["i"] + 1)
                a = act(pt.buf[:, 0:n], slot.buf[:, 0:n], ACT.Copy, tok, pt.free)
                slot.release(a)
                u["pt"], u["moved"] = pt, a
                to_c.append(u)

            def step_c():
                u = to_c.pop(0)
                slot, pt = y_ring.take(), u["pt"]
                for kb in range(u["i"] + 1):
                    v_ap, v_tok = u["v"](kb)
                    tok = mm(slot.buf[:, 0:64], pt.buf[:, kb * 128:kb * 128 + 128], v_ap, kb == 0,
                             kb == u["i"], u["moved"], v_tok, slot.free, tell=kb == u["i"])
                pt.release(tok)
                st = u["st"]
                r = st.buf[:, 2:3]
                d = DV(lambda e: e.reciprocal(r, st.buf[:, 1:2]), u["exp"])
                yt, hl, i = u["yt"], u["hl"], u["i"]
                d = ts(DV, yt.buf[:, i, 64 * hl:64 * hl + 64], slot.buf[:, 0:64], r, None, ALU.mult, None, tok, d,
                       yt.free)
                st.release(d)
                slot.release(d)
                if hl == 1 and i == 3:
                    to_d.append((yt, d, u["finish"]))

            def step_d():
                yt, d, finish = to_d.pop(0)
                slot = t_ring.take()
                for i in range(4):
                    tok = PE(lambda e, i=i, b=slot.buf: nc.tensor.transpose(
                        b[:, i * 128:i * 128 + 128], yt.buf[:, i, :], ident[:, :]), d, slot.free, tell=i == 3)
                yt.release(tok)
                slot.release(finish(slot.buf, tok))

            for ready, begin in pairs:
                while not ready():
                    yield
                heads, finish = begin()
                yt = yt_ring.take()
                for hl, (scores_of, v_of) in enumerate(heads):
                    for i in range(4):
                        if to_d:
                            step_d()
                        n = 128 * (i + 1)
                        slot, st, p = s_ring.take(), st_ring.take(), p_ring.take()
                        nb, l, mx = st.buf[:, 0:1], st.buf[:, 1:2], st.buf[:, 3:4]
                        got = scores_of(i, slot, p, mx, st.free)
                        if got[0] == "moved":
                            slot.release(got[1])
                            src = p.buf[:, 0:n]
                            d = ts(DV, nb, mx, -1.0, None, ALU.mult, None, got[1])
                        else:
                            src = slot.buf[:, 0:n]
                            d = DV(lambda e, nb=nb, src=src: e.tensor_reduce(nb, src, AX, ALU.max, negate=True),
                                   got[1], st.free)
                        a = act(p.buf[:, 0:n], src, ACT.Exp, d, p.free, bias=nb, scale=1.0, acc=l)
                        if got[0] != "moved":
                            slot.release(a)
                        to_b.append({"i": i, "hl": hl, "p": p, "exp": a, "st": st, "yt": yt, "v": v_of,
                                     "finish": finish})
                        yield
                        if len(to_b) > 1:
                            step_b()
                        if len(to_c) > 1:
                            step_c()
                        yield
            while to_b or to_c or to_d:
                if to_d:
                    step_d()
                if to_b:
                    step_b()
                    yield
                if to_c:
                    step_c()
                    yield

        def causal(slot, i, which):
            return mm(slot.buf[:, i * 128:i * 128 + 128], identb[:, 0, :], identb[:, which, :], False, True,
                      tell=True)

        fq_ring = Ring(f_qk)
        fox_in = {}
        fv_tok = []

        def fox_products(p):
            (slot,) = yield from taken(fq_ring)
            qk_free = slot.free
            toks = []

            def done(dst, k):
                def f(b, tok):
                    d = stt(DV, dst, b[:, :], k, Rb[:, :], ALU.mult, ALU.mult, tok, stat["b"], qk_free,
                            p_tok)
                    toks.append(d)
                    return d
                return f
            yield from dense("w_in", 0, cols(O_FQ + 128 * p), h, done(slot.buf[:, 0, :], 0.125))
            yield from dense("w_in", 0, cols(O_FK + 128 * p), h, done(slot.buf[:, 1, :], 1.0))
            fox_in[p] = (slot, toks)

        def fox_v(*halves):
            for c2 in halves:
                def v_out(b, tb, tok, c2=c2):
                    a = act(f_v[:, tb, c2 * 256:c2 * 256 + 256], b[:, 0:256], ACT.Copy, tok, stat["t"], p_tok,
                            scale=rtok[:, tb:tb + 1])
                    fv_tok.append(a)
                    return a
                yield from dense_tok("w_in", range(NK), cols(O_FV + 256 * c2, 256), h, v_out)

        def fox_pair(p):
            slot_in, tin = fox_in[p]

            def head(hl):
                hd = 2 * p + hl
                r = slice(64 * hl, 64 * hl + 64)
                fr_ = slice(32 * (hd % 4), 32 * (hd % 4) + 6)

                def scores(i, slot, pbuf, mx, free):
                    n = 128 * (i + 1)
                    qs = slice(i * 128, i * 128 + 128)
                    mm(slot.buf[:, 0:n], slot_in.buf[r, 0, qs], slot_in.buf[r, 1, 0:n], True, False, tin,
                       slot.free)
                    mm(slot.buf[:, 0:n], f_lq[fr_, hd // 4, qs], f_lk[fr_, hd // 4, 0:n], False, False, f_aug)
                    tok = causal(slot, i, 1)
                    if hl == 1 and i == 3:
                        slot_in.release(tok)
                    return ("psum", tok)

                def v_of(kb):
                    return f_v[:, kb, hd * 64:hd * 64 + 64], fv_tok
                return scores, v_of

            def finish(b, tok):
                assert min(p, 1) in g_last
                t1 = tmp_ring.take()
                a = act(t1.buf[:, :], b[:, :], ACT.Copy, tok, t1.free)
                e = split_act(MH[:, 4 + p, :], ML[:, 4 + p, :], t1.buf[:, :], None, a, g_last["done"])
                t1.release(e)
                mix[4 + p] = (MH[:, 4 + p, :], ML[:, 4 + p, :], e)
                return a
            return [head(0), head(1)], finish

        def chain(*gens):
            for g in gens:
                yield from g

        gla_front(0)
        pool_means()
        gen = gla_products()
        for _ in range(4):
            next(gen)
        gla_front(1)
        run(gen)
        run(fox_v(0))
        run(pool_out())
        pool_pe = [(PE.sem, PE.n)]
        run(fox_products(0))
        for s in range(2):
            p_ring.free[s] = [f_aug, tokF, pool_pe]
            pt_ring.free[s] = [f_aug, tokF, pool_pe]
        yt_ring = Ring([sub(f"f_y{i}", [128, 4, 128], F32, 84 + 2 * i) for i in range(2)], p_tok)

        sx = Sum(acc[0], [stat["b"], stat["c"]])
        h2 = [None] * 8
        hold = []

        def add_to_x(m, sum_, gname, hlist, more=None, line=None):
            def done(b, tok):
                d = tt(DV, X[:, m, :], X[:, m, :], b[:, :], ALU.add, tok)
                if sum_ is not None:
                    sum_.add(X[:, m, :], None, d, line=line)
                    if more is not None:
                        more(m, d)
                    e = split_act(HH[:, m, :], HL[:, m, :], X[:, m, :], gname(m), d, hold)
                    hlist[m] = (HH[:, m, :], HL[:, m, :], e)
                return d
            return done

        def fox_side():
            yield from fox_products(1)
            yield from fox_v(1)
            yield from fox_products(2)
            yield from gate_products()
            yield from fox_products(3)
            while 1 not in g_last:
                yield "not yet"
            yield from gla_out()
            for m in range(8):
                yield from dense("w_o", 0, cols(128 * m), mix[0:4], add_to_x(m, None, None, None))
            hold[:] = [(PE.sem, PE.n)]
            rest = [lambda k=k: mix[4 + k] for k in range(4)]
            for m in range(8):
                yield from dense("w_o", 4, cols(128 * m), rest, add_to_x(m, sx, lambda m: vec("ln2", m), h2,
                                                                          line=DV))
            wst["low"] = DV

        def with_rounds(gen, rounds):
            for x in gen:
                next(rounds, None)
                yield x
            for _ in rounds:
                yield

        wst["low"] = PO
        weave(with_rounds(attention([(lambda p=p: p in fox_in, lambda p=p: fox_pair(p)) for p in range(4)],
                                    p_ring, pt_ring, yt_ring), chain(gla_pair(0), gla_pair(1))),
              fox_side(), [1.0] * 40 + [0.65])
        hold_rb = [(DV.sem, DV.n), (AC.sem, AC.n)]

        g_ring, sg_ring, a_ring = Ring(fg), Ring(fs), Ring(fa)
        first = [True]
        ffn = {}

        def ffn_norm():
            slot, tok = total(sx)
            ffn["a"], ffn["b"] = rsqrt(Rb[:, :], slot.buf[:, :], D, tok, hold_rb)
            slot.release(ffn["a"])
        region = [(PE.sem, PE.n), (DV.sem, DV.n), (AC.sem, AC.n)]
        pending = {}
        gdown = None
        for half in range(2):
            gu = []
            for j in range(FH):
                col = (half * FH + j) * 128
                gs, ss, us = g_ring.take(), sg_ring.take(), a_ring.take()

                def gate_out(b, tok, gs=gs, ss=ss):
                    d = stt(DV, gs.buf[:, :], b[:, :], 0.5, Rb[:, :], ALU.mult, ALU.mult, tok, ffn["b"], gs.free,
                            region)
                    a = act(ss.buf[:, :], gs.buf[:, :], ACT.Tanh, d, ss.free)
                    pending["g"] = stt(DV, gs.buf[:, :], ss.buf[:, :], 1.0, gs.buf[:, :], ALU.add, ALU.mult, a)
                    ss.release(pending["g"])
                    return d

                def up_out(b, tok, gs=gs, us=us, j=j):
                    d = tt(DV, us.buf[:, :], b[:, :], Rb[:, :], ALU.mult, tok, us.free)
                    q = tt(PO, us.buf[:, :], us.buf[:, :], gs.buf[:, :], ALU.mult, d, pending["g"])
                    gs.release(q)
                    e = split_act(GH[:, j, :], GL[:, j, :], us.buf[:, :], None, q, gdown)
                    us.release(e)
                    gu.append((GH[:, j, :], GL[:, j, :], e))
                    return d
                gen = dense("w_gu", 0, cols(col), h2, gate_out)
                if first[0]:
                    first[0] = False
                    next(gen)
                    next(gen)
                    next(gen)
                    ffn_norm()
                run(gen)
                run(dense("w_gu", 0, cols(DFF + col), h2, up_out))
            if half == 0:
                for m in range(8):
                    run(dense("w_down", 0, cols(128 * m), gu, add_to_x(m, None, None, None)))
                gdown = [(PE.sem, PE.n)]
            else:
                sx = Sum(acc[0], [ffn["a"]])
                sw = Sum(acc[1], None)
                h3 = [None] * 8
                hold[:] = [(PE.sem, PE.n)]

                def gg(m):
                    return gprod[:, m:m + 1]
                gprod = rtok[:, 8:16]
                lf = VEC["ln_f"][0]
                ng = VEC["norm_g_2"][0]
                gp = tt(DV, gprod, V[:, lf:lf + 8], V[:, ng:ng + 8], ALU.mult, vtok)
                hold.append(gp)

                def more(m, d):
                    sw.add(X[:, m, :], vec("ln_f", m), d)
                for m in range(8):
                    run(dense("w_down", FH, cols(128 * m), gu, add_to_x(m, sx, gg, h3, more=more)))

        region = [(PE.sem, PE.n), (DV.sem, DV.n), (AC.sem, AC.n)]
        b2 = {}

        def norm2():
            s1, k1 = total(sx)
            s2, k2 = total(sw)
            t1 = tmp_ring.take()
            a = act(t1.buf[:, :], s1.buf[:, :], ACT.Ln, k1, t1.free, region, scale=1.0 / D, bias=eps[:, :])
            s1.release(a)
            s3, k3 = total_tok([sx, sw])
            at = act(rtok[:, 4:8], s3.buf[:, 0:4], ACT.Ln, k3, scale=1.0 / D, bias=eps[:, :])
            a2 = act(Rb[:, :], t1.buf[:, :], ACT.Exp, a, scale=-1.0)
            d = tt(DV, Rb[:, :], Rb[:, :], s2.buf[:, :], ALU.mult, a2, k2)
            s2.release(d)
            a2 = act(rtok[:, 0:4], rtok[:, 4:8], ACT.Exp, at, scale=-1.0)
            dt = tt(DV, rtok[:, 0:4], rtok[:, 0:4], s3.buf[:, 4:8], ALU.mult, a2)
            s3.release(dt)
            b2["f"] = act(Rf[:, :], t1.buf[:, :], ACT.Exp, a, scale=-0.5)
            a = act(Rb[:, :], Rb[:, :], ACT.Ln, d, scale=1.0 / D, bias=eps[:, :])
            d = tt(DV, Rb[:, :], Rb[:, :], t1.buf[:, :], ALU.add, a)
            t1.release(d)
            a = act(rtok[:, 0:4], rtok[:, 0:4], ACT.Ln, dt, scale=1.0 / D, bias=eps[:, :])
            dt = tt(DV, rtok[:, 0:4], rtok[:, 0:4], rtok[:, 4:8], ALU.add, a)
            b2["b"] = act(Rb[:, :], Rb[:, :], ACT.Exp, d, scale=-0.5)
            b2["t"] = act(rtok[:, 0:4], rtok[:, 0:4], ACT.Exp, dt, scale=-0.5)

        def scaled(dst, k, rb=None, rows=slice(0, 128), after=None, box=None, key=None, both=None):
            def done(b, tok):
                d = stt(DV, dst, b[rows, :], k, (rb or Rb)[rows, :], ALU.mult, ALU.mult, tok, b2["b"], after,
                        region)
                if box is not None:
                    box[key] = d
                return d
            return done

        ix = {}
        early = Ring([bank[0], bank[1], bank[6], bank[7]])
        early.free = dense_ring.free + y_ring.free
        waiting = []
        lo_ = landing()
        SP.dma(lo_, lambda e: e.dma_start(oh[:, :], coh), region)
        ohk = SP.dma(lo_, lambda e: e.dma_start(rbs[:, :], relb), region)
        run(dense("w_in_2", 0, cols(P_KI, 32) + cols(P_WI, 8) + (-1,) * 24 + cols(P_KR, 32)
                  + cols(P_KR + 16, 16) + cols(P_KR, 16), h3,
                  scaled(i_s[:, :], 1.0, box=ix, key="s"), ring=early, later=waiting))
        gen = dense("w_in_2", 0, cols(P_QI), h3, scaled(i_q[:, 0, :], 32.0 ** -0.5, box=ix, key="q0"),
                    ring=early, later=waiting)
        next(gen)
        norm2()
        run(gen)
        run(dense("w_in_2", 0, cols(P_QI + 128), h3, scaled(i_q[:, 1, :], 32.0 ** -0.5, box=ix, key="q1"),
                  ring=early, later=waiting))
        for finish in waiting:
            finish()
        dense_ring.free, y_ring.free = early.free[0:2], early.free[2:4]
        dense_ring.n = y_ring.n = 0

        rel = {}

        def bias_rows():
            for c in range(2):
                s = t_ring.take()
                tok = mm(s.buf[0:8, 0:320], rbs[:, :], oh[:, 320 * c:320 * c + 320], True, True, ohk, s.free,
                         tell=True)
                a = act(brow[:, 320 * c:320 * c + 320], s.buf[0:8, 0:320], ACT.Copy, tok, region)
                s.release(a)
            rel["row"] = SP.dma(landing(), lambda e: e.dma_start(scratch[:, 0, :], brow[:, :]), a)

        def bias_copies(*heads):
            for hd in heads:
                src = scratch[hd:hd + 1, 0, :]
                src = bass.AP(tensor=src.tensor, offset=src.offset, ap=[[0, 127], [1, REL]])
                rel[hd] = SP.dma(landing(), lambda e, hd=hd, src=src: e.dma_start(scratch[hd, 1:128, :], src),
                                 rel["row"])

        lk = landing()
        for g in range(4):
            ktok = SP.dma(lk, lambda e, g=g: e.dma_start(i_k[32 * g:32 * g + 32, :], i_s[0:32, :]), ix["s"],
                          region)
        ix["k"] = ktok
        t1, t2 = tmp_ring.take(), tmp_ring.take()
        d1 = tt(DV, t1.buf[64:96, :], i_s[64:96, :], RT[64:96, :], ALU.mult, ix["s"], consts, t1.free)
        d2 = tt(DV, t2.buf[64:96, :], i_s[96:128, :], RT[96:128, :], ALU.mult, t2.free)
        akr = []
        for s_ in range(4):
            akr.append(tt(DV, a_k[s_][64:96, :], t1.buf[64:96, :], t2.buf[64:96, :], ALU.add, d1, d2, region))
        akr = [tt(DV, a_k[s_][96:128, :], t1.buf[64:96, :], t2.buf[64:96, :], ALU.add, d1, d2, region)
               for s_ in range(4)][-1]
        t1.release(akr)
        t2.release(akr)
        off = {1: 0, 2: 256, 3: 640}

        tops = behind["gens"]
        behind["per"] = 1.1

        def index_scores():
            for i in (3, 2, 1):
                n = 128 * (i + 1)
                sc = score[:, off[i]:off[i] + n]
                prev = None
                for hd in range(8):
                    r = slice(32 * (hd % 4), 32 * (hd % 4) + 32)
                    slot = s_ring.take()
                    tok = mm(slot.buf[:, 0:n], i_q[r, hd // 4, i * 128:i * 128 + 128], i_k[r, 0:n], True, True,
                             ix["k"], ix[f"q{hd // 4}"], slot.free, tell=True)
                    t = sq_ring.take()
                    a = act(t.buf[:, 0:n], slot.buf[:, 0:n], ACT.Relu, tok, t.free)
                    slot.release(a)
                    w = wi[:, i, hd:hd + 1]
                    if prev is None:
                        prev = ts(DV, sc, t.buf[:, 0:n], w, None, ALU.mult, None, a, ix["w"], region)
                    else:
                        prev = stt(DV, sc, t.buf[:, 0:n], w, sc, ALU.mult, ALU.add, a, prev)
                    t.release(prev)
                    yield
                prev = DV(lambda e, i=i, n=n: e.memset(score[0:64, off[i] + n - 64:off[i] + n], -BIG), prev)
                tops.append(top(i, n, sc, prev))

        def top(i, n, sc, prev):
            for rnd in range(16):
                d = DV(lambda e: e.max(m8[:, :], sc), prev)
                prev = DV(lambda e: e.match_replace(sc, m8[:, :], sc, GONE), d)
                yield
            ix[f"m{i}"] = ts(DV, nmask[:, off[i]:off[i] + n], sc, -2.0e38, -BIG, ALU.is_gt, ALU.mult, prev)

        slq, slk = Sum(acc[0], [(PE.sem, PE.n)]), Sum(acc[1], [(PE.sem, PE.n)])
        lq, lk_ = [], []

        def lat_out(c, hi, lo, gname, sum_, lst):
            def done(b, tok):
                t = tmp_ring.take()
                d = tt(DV, t.buf[:, :], b[:, :], Rb[:, :], ALU.mult, tok, b2["b"], t.free)
                s = sum_.add(t.buf[:, :], None, d)
                e = split_act(hi[:, c, :], lo[:, c, :], t.buf[:, :], vec(gname, c), d, region)
                t.release(e, s)
                lst.append((hi[:, c, :], lo[:, c, :], e))
                return d
            return done

        la = {}

        def latents():
            for c in range(2):
                yield from dense("w_in_2", 0, cols(P_CKV + 128 * c), h3,
                                 lat_out(c, LKH, LKL, "g_kv_lat_2", slk, lk_))
            bias_rows()
            bias_copies(0, 1)
            for c in range(3):
                yield from dense("w_in_2", 0, cols(P_QL + 128 * c), h3, lat_out(c, LQH, LQL, "g_q_lat_2", slq, lq))
                if c == 0:
                    kv_norm()
            gen = z_products(P_ZA, za_in, 0)
            for n, _ in enumerate(gen):
                if n == 2:
                    q_norm()
                yield

        def q_norm():
            s, k = total(slq)
            a, d = rsqrt(RQ[:, :], s.buf[:, :], 384, k, region)
            s.release(a)
            la["q"] = tt(DV, RQ[64:128, :], RQ[64:128, :], RT[64:128, :], ALU.mult, d)

        def kv_norm():
            s1, k1 = total(slk)
            s2, k2 = total_tok([slk])
            a1 = act(RK[:, :], s1.buf[:, :], ACT.Ln, k1, region, scale=1.0 / 256, bias=eps[:, :])
            a2 = act(rtok[:, 4:8], s2.buf[:, 0:4], ACT.Ln, k2, b2["t"], scale=1.0 / 256, bias=eps[:, :])
            s1.release(a1)
            s2.release(a2)
            la["k"] = act(RK[:, :], RK[:, :], ACT.Exp, a1, scale=-0.5)
            la["t"] = act(rtok[:, 4:8], rtok[:, 4:8], ACT.Exp, a2, scale=-0.5)

        va_tok = []

        def mla_v():
            while tile_no[0] % 2:
                _, _, _, t = next_tile((None, 0, ()))
                tile_done(t, wst["last_pe"])
            tiles, starts = [], []
            for c2 in range(2):
                column = sum((cols(hd * 128 + 64, 64) for hd in range(4 * c2, 4 * c2 + 4)), ())
                for k in range(2):
                    a = next_tile(("w_ukv_2", k, column[:128]))
                    next_tile(("w_ukv_2", k, column[128:]))
                    starts.append(a[3])
                    j, c = (a[3] // UT) % NW, (a[3] % UT) * 128
                    tiles.append((WH[:, j, c:c + 256], WL[:, j, c:c + 256], a[2]))
            for tb in range(4):
                slot = dense_ring.take()
                for i, (wh, wl, ready) in enumerate(tiles):
                    hh, hl, tok = lk_[i % 2]
                    hh, hl = hh[:, tb * 128:tb * 128 + 128], hl[:, tb * 128:tb * 128 + 128]
                    first, last = i % 2 == 0, i % 2 == 1
                    out = slot.buf[:, 256 * (i // 2):256 * (i // 2) + 256]
                    mm(out, hh, wh, first, False, slot.free, ready, tok)
                    mm(out, hh, wl, False, False)
                    tok2 = mm(out, hl, wh, False, last, tell=i == 3)
                a = act(a_v[:, tb, :], slot.buf[:, :], ACT.Copy, tok2, la["t"], region, scale=rtok[:, 4 + tb:5 + tb])
                va_tok.append(a)
                slot.release(a)
                if tb == 3:
                    wst["last_pe"] = tok2
                    for t in starts:
                        tile_done(t, tok2)
                        tile_done(t + 1, tok2)
                yield

        aq_ring = Ring(a_q)
        mla_in = {}
        z_ring = Ring(zb)

        def z_products(col, box, p):
            (z,) = yield from taken(z_ring)
            bx = {}
            yield from dense("w_in_2", 0, cols(col + 128 * p), h3, scaled(z.buf[:, :], 0.5, after=z.free, box=bx,
                                                                          key="z"))
            box[p] = (z, silu_in_place(z.buf[:, :], bx["z"], tmp_ring))

        za_in, zb_in = {}, {}

        def mla_products(p):
            sl = yield from taken(aq_ring, 2)
            tk = []

            def q_out(slot):
                def f(b, tok):
                    d = stt(DV, slot.buf[:, :], b[:, :], 96.0 ** -0.5, RQ[:, :], ALU.mult, ALU.mult, tok, la["q"],
                            slot.free, region)
                    tk.append(d)
                    return d
                return f

            def k_out(b, tok):
                for hl in range(2):
                    r = slice(64 * hl, 64 * hl + 64)
                    d = tt(DV, a_k[sl[hl].i][0:64, :], b[r, :], RK[r, :], ALU.mult, tok, la["k"], sl[hl].free)
                    tk.append(d)
                return d
            yield from dense("w_ukv_2", 0, cols(256 * p, 64) + cols(256 * p + 128, 64), lk_, k_out)
            for hl in range(2):
                hd = 2 * p + hl
                yield from dense("w_uq_2", 0, cols(96 * hd, 96) + cols(96 * hd + 80, 16) + cols(96 * hd + 64, 16),
                                 lq, q_out(sl[hl]))
            if p:
                yield from z_products(P_ZA, za_in, p)
            mla_in[p] = (sl, tk)

        ya, yb = [None] * 4, [None] * 4

        def gated(p, hi, lo, lst, box):
            def finish(b, tok):
                z, ztok = box[p]
                t1 = tmp_ring.take()
                d = tt(DV, t1.buf[:, :], b[:, :], z.buf[:, :], ALU.mult, tok, ztok, t1.free)
                z.release(d)
                e = split_act(hi[:, p, :], lo[:, p, :], t1.buf[:, :], None, d, region, rel["row"])
                t1.release(e)
                lst[p] = (hi[:, p, :], lo[:, p, :], e)
                return d
            return finish

        def mla_pair(p):
            sl, tin = mla_in[p]

            def head(hl):
                hd = 2 * p + hl
                q, k = sl[hl].buf, a_k[sl[hl].i]

                def scores(i, slot, pbuf, mx, free):
                    n = 128 * (i + 1)
                    mm(slot.buf[:, 0:n], q[:, i * 128:i * 128 + 128], k[:, 0:n], True, False, tin, akr, slot.free)
                    tok = causal(slot, i, 2)
                    if i == 3:
                        sl[hl].release(tok)
                    return ("psum", tok)

                def v_of(kb):
                    return a_v[:, kb, hd * 64:hd * 64 + 64], va_tok
                return scores, v_of
            return [head(0), head(1)], gated(p, YAH, YAL, ya, za_in)

        wst["low"] = PO
        side = chain(latents(), mla_v(), mla_products(0))
        for _ in range(6):
            next(side)
        s = t_ring.take()
        for tb in range(4):
            tok = PE(lambda e, tb=tb, b=s.buf: nc.tensor.transpose(
                b[:, 8 * tb:8 * tb + 8], i_s[32:40, tb * 128:tb * 128 + 128], ident[32:40, 32:40]),
                ix["s"], s.free, tell=tb == 3)
        ix["w"] = act(wi[:, :, :].rearrange("p a b -> p (a b)"), s.buf[:, 0:32], ACT.Copy, tok,
                      scale=8.0 ** -0.5)
        s.release(ix["w"])
        weave(index_scores(), side, 1.0)
        pc_ring, ptc_ring = Ring(Pc, region), Ring(PTc, region)
        yt3_free = [(PE.sem, PE.n), (DV.sem, DV.n), (AC.sem, AC.n), ktok]
        yt3_ring = Ring([sub(f"b_y{i}", [128, 4, 128], F32, 2 * i) for i in range(2)], yt3_free)

        b_ring = Ring(b_qk)
        dsa_in = {}
        bv_tok = []
        hold3 = []

        def dsa_v():
            hold3[:] = [(PE.sem, PE.n)]
            for c2 in range(2):
                def v_out(b, tb, tok, c2=c2):
                    a = act(b_v[:, tb, c2 * 256:c2 * 256 + 256], b[:, 0:256], ACT.Copy, tok, b2["t"], hold3,
                            scale=rtok[:, tb:tb + 1])
                    bv_tok.append(a)
                    return a
                yield from dense_tok("w_in_2", range(NK), cols(P_VB + 256 * c2, 256), h3, v_out)

        bias_in = {}
        t_land = [landing(), landing()]
        t_bias = Ring(b_t)

        def dsa_bias(hd):
            if hd > 7:
                return
            bs = t_bias.take()
            src = scratch[hd:hd + 1, 0, :]
            ap = bass.AP(tensor=src.tensor, offset=src.offset + 127, ap=[[REL - 1, 128], [1, T]])
            bias_in[hd] = (bs, SP.dma(t_land[hd % 2], lambda e, bs=bs, ap=ap: e.dma_start(bs.buf[:, :], ap),
                                      bs.free, rel[hd], hold3))

        def dsa_products(p):
            (s,) = yield from taken(b_ring)
            bx = {}
            yield from dense("w_in_2", 0, cols(P_QB + 128 * p), h3,
                             scaled(s.buf[:, 0, :], 0.125, after=[s.free, hold3], box=bx, key="q"))
            yield from dense("w_in_2", 0, cols(P_KB + 128 * p), h3,
                             scaled(s.buf[:, 1, :], 1.0, after=[s.free, hold3], box=bx, key="k"))
            dsa_in[p] = (s, [bx["q"], bx["k"]])
            yield from z_products(P_ZB, zb_in, p)

        def dsa_pair(p):
            s, tin = dsa_in[p]

            def head(hl):
                hd = 2 * p + hl
                r = slice(64 * hl, 64 * hl + 64)

                def scores(i, slot, pbuf, mx, free):
                    bs, bt = bias_in[hd]
                    n = 128 * (i + 1)
                    mm(slot.buf[:, 0:n], s.buf[r, 0, i * 128:i * 128 + 128], s.buf[r, 1, 0:n], True, False, tin,
                       slot.free)
                    if i == 0:
                        tok = causal(slot, 0, 2)
                    else:
                        tok = mm(slot.buf[:, 0:n], identb[:, 0, :], nmask[:, off[i]:off[i] + n], False, True,
                                 ix[f"m{i}"], tell=True)
                    d = DV(lambda e: e.tensor_tensor_reduce(
                        out=pbuf.buf[:, 0:n], in0=slot.buf[:, 0:n], in1=bs.buf[:, 512 - n:512], scale=1.0,
                        scalar=GONE, op0=ALU.add, op1=ALU.max, accum_out=mx), tok, bt, pbuf.free, free)
                    if i == 3:
                        bs.release(d)
                        if hl == 1:
                            s.release(tok)
                    if i == 0:
                        dsa_bias(hd + 1)
                    return ("moved", d)

                def v_of(kb):
                    return b_v[:, kb, hd * 64:hd * 64 + 64], bv_tok
                return scores, v_of
            return [head(0), head(1)], gated(p, YBH, YBL, yb, zb_in)

        def mla_side():
            for p in range(1, 4):
                bias_copies(2 * p, 2 * p + 1)
                yield from mla_products(p)
            yield from dsa_v()
            dsa_bias(0)
            yield from dsa_products(0)
            for p in range(1, 4):
                yield from dsa_products(p)
            held = [(DV.sem, DV.n)]
            ga = Ring(acc, held)
            rest = [lambda k=k: ya[k] for k in range(4)]
            for m in range(8):
                yield from gated_product(m, "w_o_a_2", P_GA, rest, ga.take(), a_half[m], held, a_toks)

        def dsa_ready():
            if 0 not in dsa_in or 0 not in zb_in:
                return False
            if tops and next(tops[0], "end") == "end":
                tops.pop(0)
            return not tops

        a_toks = []
        a_half = [sub(f"a_h{i}", [128, T], F32, at_) for i, at_ in enumerate((8, 10, 88, 90, 68, 70, 72, 74))]

        def gated_product(m, mat, col, y, g, q, free, toks):
            bx = {}

            def g_out(b, tok):
                d = stt(DV, g.buf[:, :], b[:, :], 0.5, Rb[:, :], ALU.mult, ALU.mult, tok, g.free)
                bx["g"] = act(g.buf[:, :], g.buf[:, :], ACT.Tanh, d)
                return d

            def y_out(b, tok):
                d = stt(DV, q[:, :], g.buf[:, :], 1.0, b[:, :], ALU.add, ALU.mult, tok, bx["g"], free)
                g.release(d)
                toks.append(d)
                return d
            yield from dense("w_in_2", 0, cols(col + 128 * m), h3, g_out)
            yield from dense(mat, 0, cols(128 * m), y, y_out)

        side = mla_side()
        for _ in range(3):
            next(side)
        weave(attention([(lambda p=p: p in mla_in, lambda p=p: mla_pair(p)) for p in range(4)]
                        + [(lambda p=p: p in zb_in and dsa_ready(), lambda p=p: dsa_pair(p)) for p in range(4)],
                        pc_ring, ptc_ring, yt3_ring), side, [0.9] * 66 + [0.85])

        late = [(PE.sem, PE.n), (DV.sem, DV.n), (AC.sem, AC.n)]
        wst["low"] = DV
        gt = Ring([Pc[0], Pc[1], PTc[0], PTc[1]], late)
        mt = Ring(zb, late)
        merged = []
        for m in range(8):
            q, qa, b_tok = mt.take(), a_half[m], []
            run(gated_product(m, "w_o_b_2", P_GB, yb, gt.take(), q.buf, q.free, b_tok))
            d = tt(PO, q.buf[:, :], qa[:, :], q.buf[:, :], ALU.add, a_toks[m], b_tok)
            e = split_act(MGH[:, m, :], MGL[:, m, :], q.buf[:, :], 0.5, d, late)
            q.release(e)
            merged.append((MGH[:, m, :], MGL[:, m, :], e))
            b2[f"x{m}"] = stt(DV, X[:, m, :], X[:, m, :], vec("ln_f", m), Rf[:, :], ALU.mult, ALU.mult, b2["f"])

        sx = Sum(acc[0], late)
        late = [(PE.sem, PE.n), (DV.sem, DV.n), (AC.sem, AC.n)]
        scaled_x, last = [], {}
        o_x = sub("o_x", [128, 3, T], F32, 32)
        for m in range(8):
            def done(b, tok, m=m):
                d = tt(DV, X[:, m, :], X[:, m, :], b[:, :], ALU.add, tok, b2[f"x{m}"])
                if m < 7:
                    sx.add(X[:, m, :], None, d, line=DV)
                else:
                    last["q"] = sq_ring.take()
                    last["t"] = act(last["q"].buf[:, :], X[:, m, :], ACT.Square, d, last["q"].free)
                if m < 3:
                    scaled_x.append(act(o_x[:, m, :], X[:, m, :], ACT.Copy, d, late, scale=vec("final_g_2", m)))
                return d
            if m == 7:
                act(small[:, 0:1], eps[:, :], ACT.Ln, late)
            run(dense("w_out_2", 0, cols(128 * m), merged, done))
        s = t_ring.take()
        mm(s.buf[:, :], ones[:, :], sx.buf[:, :], True, False, sx.tok, s.free)
        k = mm(s.buf[:, :], ones[:, :], last["q"].buf[:, :], False, True, last["t"], tell=True)
        a, b = rsqrt(Rb[:, :], s.buf[:, :], D, k)
        s.release(a)
        lout = landing()
        for m in range(8):
            if m in (0, 3, 6):
                c = m // 3
                d = tt(PO, o_x[:, c, :], o_x[:, c, :], Rb[:, :], ALU.mult, b, scaled_x[c])
                fin = SP.dma(lout, lambda e, c=c: e.dma_start(outT[:, c, :], o_x[:, c, :]), d)
                continue
            m = {1: 3, 2: 4, 4: 5, 5: 6, 7: 7}[m]
            d = stt(DV, X[:, m, :], X[:, m, :], vec("final_g_2", m), Rb[:, :], ALU.mult, ALU.mult, b)
            fin = SP.dma(lout, lambda e, m=m: e.dma_start(outT[:, m, :], X[:, m, :]), d)
        SP.todo.append(([fin, rel["row"], *(rel[hd] for hd in range(8))], lambda e: None, None))
        while tile_no[0] < NTILES:
            tile_no[0] += 1
            plan.append((None, 0, ()))
        assert tile_no[0] == NTILES, tile_no

        block = ctx.enter_context(nc.Block())

        @block.sync
        def _(eng):
            SP.emit(eng)

        @block.scalar
        def _(eng):
            AC.emit(eng)

        @block.vector
        def _(eng):
            DV.emit(eng)

        @block.gpsimd
        def _(eng):
            PO.emit(eng)

        @block.tensor
        def _(eng):
            PE.emit(eng)
    return plan


def rope_table():
    half = 16
    freqs = np.float32(10000.0) ** (-np.arange(half, dtype=np.float32) / np.float32(half))
    ang = np.arange(T, dtype=np.float32)[:, None] * freqs.astype(np.float32)[None, :]
    cos, sin = np.cos(ang).T.astype(np.float32), np.sin(ang).T.astype(np.float32)
    out = np.ones((128, T), np.float32)
    out[64:80], out[80:96], out[96:112], out[112:128] = cos, cos, -sin, sin
    return out


def bucket_of(rel):
    nb, exact = 16, 8
    ret = (rel > 0).astype(np.int32) * nb
    n = np.abs(rel)
    nf = np.maximum(n, 1).astype(np.float32)
    large = exact + (np.log(nf / np.float32(exact)) / np.float32(np.log(128 / exact))
                     * np.float32(nb - exact)).astype(np.int32)
    large = np.minimum(large, nb - 1)
    return ret + np.where(n < exact, n, large)


def constants():
    p = np.arange(128)
    cf = np.zeros((128, 896), np.float32)
    cf[:, 0:128] = np.eye(128, dtype=np.float32)
    cf[:, 128:640] = rope_table()
    keep = (p % 64)[:, None] <= np.arange(64)[None, :]
    cf[:, 640:704] = np.where(keep, np.float32(3.0e38), np.float32(0))
    cf[:, 704:768] = np.where(keep, np.float32(-3.0e38), np.float32(0))
    cf[:, 768:896] = (p[:, None] // 64 == p[None, :] // 64)
    cph = np.zeros((128, 1536), np.float32)
    t1 = np.arange(1, T + 1)
    for g, w in enumerate((2, 4, 8, 16)):
        r = slice(64 * (g % 2), 64 * (g % 2) + 64)
        cph[r, 512 * (g // 2):512 * (g // 2) + 512] = np.float32(1) / np.minimum(t1, w).astype(np.float32)
    cph[:, 1024:1536] = (np.arange(T) % 64 != 0)
    coh = np.zeros((32, REL), np.float32)
    for n in range(REL - 1):
        coh[bucket_of(np.array(n - 127 - 384))[()], n] = 1.0
    coh[0, REL - 1] = 1.0
    from concourse import mybir as _mybir
    cb = np.zeros((128, 3, 128), np.float32)
    cb[:, 0] = np.eye(128)
    cb[:, 1] = np.where(p[None, :] <= p[:, None], 0.0, -BIG)
    cb[:, 2] = np.where(p[None, :] // 64 <= p[:, None] // 64, 0.0, -BIG)
    return cf, cph, coh, cb.astype(_mybir.dt.np(_mybir.dt.bfloat16))


def kernel(**inputs):
    import concourse.bacc as _bacc
    from concourse.bass_utils import run_bass_kernel_spmd as _run

    a = {k: np.asarray(v) for k, v in inputs.items()}
    nc = _bacc.Bacc("TRN2", target_bir_lowering=False, num_devices=1)
    arrays, order = {}, []

    def give(name, shape, dt):
        ap = nc.dram_tensor(name, shape, dt, kind="ExternalInput").ap()
        order.append(name)
        return ap

    NU = NTILES // UT
    wall = give("wall", (NU, 128, UT * 128), F32)
    xT = give("xT", (128, NK, T), F32)
    vecs = give("vecs", (128, NVEC), F32)
    wa = give("wa", (16, 256), F32)
    wp = give("wp", (128, 2, 128), F32)
    relb = give("relb", (32, 8), F32)
    cf = give("cf", (128, 896), F32)
    cph = give("cph", (128, 1536), F32)
    coh = give("coh", (32, REL), F32)
    cb = give("cb", (128, 3, 128), BF16)
    scratch = nc.dram_tensor("scratch", (8, 128, REL), F32, kind="Internal").ap()
    outT = nc.dram_tensor("outT", (128, NK, T), F32, kind="ExternalOutput").ap()
    plan = build(nc, wall, xT, vecs, wa, wp, relb, cf, cph, coh, cb, scratch, outT)

    w = np.zeros((NTILES, 128, 128), np.float32)
    for t, (name, k, column) in enumerate(plan):
        if name is None:
            continue
        m = a[name][0]
        c = np.array(column)
        have = c >= 0
        w[t][:, have] = m[128 * k:128 * k + 128][:, c[have]]
    arrays["wall"] = np.ascontiguousarray(w.reshape(NU, UT, 128, 128).transpose(0, 2, 1, 3)).reshape(
        NU, 128, UT * 128)
    arrays["xT"] = np.ascontiguousarray(a["x"][0].T.reshape(NK, 128, T).transpose(1, 0, 2))
    v = np.zeros((128, NVEC), np.float32)
    for name, (at, n) in VEC.items():
        g = a[name].reshape(-1)
        if name == "b_f":
            v[32:40, at] = g
        else:
            v[:, at:at + n] = g.reshape(n, 128).T
    arrays["vecs"] = v
    arrays["wa"] = np.ascontiguousarray(a["w_a_up"][0])
    wpp = np.zeros((128, 2, 128), np.float32)
    for g in range(4):
        r = slice(64 * (g % 2), 64 * (g % 2) + 64)
        wpp[r, g // 2, r] = a["w_pool"][0, g]
    arrays["wp"] = wpp
    arrays["relb"] = np.ascontiguousarray(a["rel_bias_2"])
    arrays["cf"], arrays["cph"], arrays["coh"], arrays["cb"] = constants()
    r = _run(nc, [arrays], core_ids=[0])
    y = r.results[0]["outT"]
    return np.ascontiguousarray(y.transpose(1, 0, 2).reshape(D, T).T)[None]
```
